# Optimizing a Trainium2 kernel written in Bass

```python
import math
import jax, jax.numpy as jnp
from jax import lax
import numpy as np

D_MODEL = 1024
BATCH = 1
SEQ = 256
DEPTH = 2

D_INNER = 2 * D_MODEL
SSM_WIDTH = D_INNER // 2
RET_WIDTH = D_INNER - SSM_WIDTH
SSM_HEAD_DIM = 64
SSM_HEADS = SSM_WIDTH // SSM_HEAD_DIM
SSM_GROUPS = 2
SSM_STATE = 128
CONV_K = 4
CONV_DIM = SSM_WIDTH + 2 * SSM_GROUPS * SSM_STATE
SSM_CHUNK = 128
RET_HEADS = 4
RET_V_DIM = RET_WIDTH // RET_HEADS
RET_QK_DIM = RET_V_DIM // 2
RET_CHUNK = 128
ROPE_BASE = 10000.0
D_FF = 2816
IN_PROJ_DIM = SSM_WIDTH + CONV_DIM + SSM_HEADS + 2 * RET_HEADS * RET_QK_DIM + 2 * RET_WIDTH
NORM_EPS = 1e-6

kernel_name = "hybrid_ssd_retention_macaron_sandwich"

def rms_norm(x, w):
    xf = x.astype(jnp.float32)
    y = xf * lax.rsqrt(jnp.mean(xf * xf, axis=-1, keepdims=True) + NORM_EPS)
    return (y * w.astype(jnp.float32)).astype(x.dtype)

def swiglu(x, w_in, w_out):
    gate, up = jnp.split(x @ w_in, 2, axis=-1)
    return (jax.nn.silu(gate) * up) @ w_out

def to_chunks(a, ch):
    b, s = a.shape[:2]
    return jnp.moveaxis(a.reshape(b, s // ch, ch, *a.shape[2:]), 1, 0)

def from_chunks(a):
    a = jnp.moveaxis(a, 0, 1)
    return a.reshape(a.shape[0], a.shape[1] * a.shape[2], *a.shape[3:])

def causal_depthwise_conv(x, w, bias):
    y = lax.conv_general_dilated(
        x, w[:, None, :].astype(x.dtype), window_strides=(1,),
        padding=[(CONV_K - 1, 0)], dimension_numbers=("NWC", "WIO", "NWC"),
        feature_group_count=x.shape[-1])
    return y + bias.astype(x.dtype)

def ssd_chunked(xdt, dta, bm, cm):
    b, s = xdt.shape[:2]
    e = SSM_HEADS // SSM_GROUPS
    xs = to_chunks(xdt.reshape(b, s, SSM_GROUPS, e, SSM_HEAD_DIM), SSM_CHUNK)
    as_ = to_chunks(dta.reshape(b, s, SSM_GROUPS, e), SSM_CHUNK)
    bs = to_chunks(bm, SSM_CHUNK)
    cs = to_chunks(cm, SSM_CHUNK)
    causal = jnp.tril(jnp.ones((SSM_CHUNK, SSM_CHUNK), dtype=bool))[None, :, :, None, None]

    def step(state, inp):
        xc, ac, bc, cc = inp
        acum = jnp.cumsum(ac, axis=1)
        diff = acum[:, :, None] - acum[:, None, :]
        lmat = jnp.exp(jnp.where(causal, diff, -jnp.inf))
        cb = jnp.einsum("btgn,bsgn->btsg", cc, bc)
        y_intra = jnp.einsum("btsg,btsge,bsgep->btgep", cb, lmat, xc)
        y_inter = jnp.einsum("btgn,bgepn->btgep", cc, state) * jnp.exp(acum)[..., None]
        decay_to_end = jnp.exp(acum[:, -1:] - acum)
        new_state = state * jnp.exp(acum[:, -1])[..., None, None] + jnp.einsum(
            "bsgn,bsge,bsgep->bgepn", bc, decay_to_end, xc)
        return new_state, y_intra + y_inter

    init = jnp.zeros((b, SSM_GROUPS, e, SSM_HEAD_DIM, SSM_STATE), jnp.float32)
    _, ys = lax.scan(step, init, (xs, as_, bs, cs))
    return from_chunks(ys).reshape(b, s, SSM_HEADS, SSM_HEAD_DIM)

def retention_chunked(q, k, v):
    b = q.shape[0]
    log_gamma = jnp.log(1.0 - 2.0 ** (-5.0 - jnp.arange(RET_HEADS, dtype=jnp.float32)))
    pos = jnp.arange(RET_CHUNK, dtype=jnp.float32)
    rel = pos[:, None] - pos[None, :]
    dmat = jnp.exp(jnp.where((rel >= 0)[None], rel[None] * log_gamma[:, None, None], -jnp.inf))
    q_decay = jnp.exp((pos[:, None] + 1.0) * log_gamma[None])
    k_decay = jnp.exp((RET_CHUNK - 1.0 - pos[:, None]) * log_gamma[None])
    chunk_decay = jnp.exp(RET_CHUNK * log_gamma)

    def step(state, inp):
        qc, kc, vc = inp
        scores = jnp.einsum("bthd,bshd->bhts", qc, kc) * dmat
        y = jnp.einsum("bhts,bshe->bthe", scores, vc) + jnp.einsum(
            "bthd,bhde->bthe", qc, state) * q_decay[None, :, :, None]
        new_state = state * chunk_decay[None, :, None, None] + jnp.einsum(
            "bshd,bshe,sh->bhde", kc, vc, k_decay)
        return new_state, y

    init = jnp.zeros((b, RET_HEADS, RET_QK_DIM, RET_V_DIM), jnp.float32)
    _, ys = lax.scan(step, init, (to_chunks(q, RET_CHUNK), to_chunks(k, RET_CHUNK), to_chunks(v, RET_CHUNK)))
    return from_chunks(ys)

def rotary(x, positions):
    half = x.shape[-1] // 2
    inv_freq = ROPE_BASE ** (-jnp.arange(half, dtype=jnp.float32) / half)
    ang = positions.astype(jnp.float32)[..., None] * inv_freq
    cos = jnp.cos(ang)[:, :, None, :]
    sin = jnp.sin(ang)[:, :, None, :]
    x1, x2 = x[..., :half], x[..., half:]
    return jnp.concatenate([x1 * cos - x2 * sin, x1 * sin + x2 * cos], axis=-1)

def hybrid_mixer(u, positions, w_in, conv_w, conv_b, dt_bias, a_log, d_skip, ssm_norm, ret_norm, w_out):
    b, s, _ = u.shape
    f32 = jnp.float32
    sizes = [SSM_WIDTH, CONV_DIM, SSM_HEADS, RET_HEADS * RET_QK_DIM, RET_HEADS * RET_QK_DIM, RET_WIDTH, RET_WIDTH]
    split_at = np.cumsum(sizes)[:-1].tolist()
    z, xbc, dt, q, k, v, g = jnp.split(u @ w_in, split_at, axis=-1)

    xbc = jax.nn.silu(causal_depthwise_conv(xbc, conv_w, conv_b))
    xs, bm, cm = jnp.split(xbc.astype(f32), [SSM_WIDTH, SSM_WIDTH + SSM_GROUPS * SSM_STATE], axis=-1)
    xs = xs.reshape(b, s, SSM_HEADS, SSM_HEAD_DIM)
    bm = bm.reshape(b, s, SSM_GROUPS, SSM_STATE)
    cm = cm.reshape(b, s, SSM_GROUPS, SSM_STATE)
    dt = jax.nn.softplus(dt.astype(f32) + dt_bias.astype(f32))
    a = -jnp.exp(a_log.astype(f32))
    y = ssd_chunked(xs * dt[..., None], dt * a, bm, cm) + xs * d_skip.astype(f32)[:, None]
    y_ssm = rms_norm(y.reshape(b, s, SSM_WIDTH) * jax.nn.silu(z.astype(f32)), ssm_norm)

    q = rotary(q.astype(f32).reshape(b, s, RET_HEADS, RET_QK_DIM), positions)
    k = rotary(k.astype(f32).reshape(b, s, RET_HEADS, RET_QK_DIM), positions) * (RET_QK_DIM ** -0.5)
    v = v.astype(f32).reshape(b, s, RET_HEADS, RET_V_DIM)
    r = retention_chunked(q, k, v)
    mu = jnp.mean(r, axis=-1, keepdims=True)
    var = jnp.mean(jnp.square(r - mu), axis=-1, keepdims=True)
    r = (r - mu) * lax.rsqrt(var + 1e-5) * ret_norm.astype(f32).reshape(RET_HEADS, RET_V_DIM)
    y_ret = jax.nn.silu(g.astype(f32)) * r.reshape(b, s, RET_WIDTH)

    return jnp.concatenate([y_ssm.astype(f32), y_ret], axis=-1).astype(u.dtype) @ w_out

def setup_inputs(seed: int = 0) -> dict:
    key = jax.random.key(seed)
    ks = iter(jax.random.split(key, 32))
    f32 = jnp.float32
    L = DEPTH

    def normal(shape, scale):
        return jax.random.normal(next(ks), shape, f32) * scale

    def gain(shape):
        return 1.0 + 0.02 * jax.random.normal(next(ks), shape, f32)

    x = jax.random.normal(next(ks), (BATCH, SEQ, D_MODEL), f32)
    positions = jnp.broadcast_to(jnp.arange(SEQ, dtype=jnp.int32)[None], (BATCH, SEQ))
    dt0 = jnp.exp(jax.random.uniform(next(ks), (L, SSM_HEADS), f32, math.log(1e-3), math.log(1e-1)))
    dt_bias = dt0 + jnp.log(-jnp.expm1(-dt0))
    a_log = jnp.log(jax.random.uniform(next(ks), (L, SSM_HEADS), f32, 1.0, 16.0))
    return {
        "x": x,
        "positions": positions,
        "ffn1_pre_norm": gain((L, D_MODEL)),
        "ffn1_w_in": normal((L, D_MODEL, 2 * D_FF), D_MODEL ** -0.5),
        "ffn1_w_out": normal((L, D_FF, D_MODEL), D_FF ** -0.5),
        "ffn1_post_norm": gain((L, D_MODEL)),
        "mix_pre_norm": gain((L, D_MODEL)),
        "mix_w_in": normal((L, D_MODEL, IN_PROJ_DIM), D_MODEL ** -0.5),
        "conv_w": normal((L, CONV_K, CONV_DIM), CONV_K ** -0.5),
        "conv_b": normal((L, CONV_DIM), 0.02),
        "dt_bias": dt_bias,
        "a_log": a_log,
        "d_skip": gain((L, SSM_HEADS)),
        "ssm_norm": gain((L, SSM_WIDTH)),
        "ret_norm": gain((L, RET_WIDTH)),
        "mix_w_out": normal((L, D_INNER, D_MODEL), D_INNER ** -0.5),
        "mix_post_norm": gain((L, D_MODEL)),
        "ffn2_pre_norm": gain((L, D_MODEL)),
        "ffn2_w_in": normal((L, D_MODEL, 2 * D_FF), D_MODEL ** -0.5),
        "ffn2_w_out": normal((L, D_FF, D_MODEL), D_FF ** -0.5),
        "ffn2_post_norm": gain((L, D_MODEL)),
    }

def reference(x, positions, ffn1_pre_norm, ffn1_w_in, ffn1_w_out, ffn1_post_norm,
              mix_pre_norm, mix_w_in, conv_w, conv_b, dt_bias, a_log, d_skip, ssm_norm, ret_norm,
              mix_w_out, mix_post_norm, ffn2_pre_norm, ffn2_w_in, ffn2_w_out, ffn2_post_norm):
    for l in range(DEPTH):
        x = x + 0.5 * rms_norm(swiglu(rms_norm(x, ffn1_pre_norm[l]), ffn1_w_in[l], ffn1_w_out[l]), ffn1_post_norm[l])
        mixed = hybrid_mixer(rms_norm(x, mix_pre_norm[l]), positions, mix_w_in[l], conv_w[l], conv_b[l],
                             dt_bias[l], a_log[l], d_skip[l], ssm_norm[l], ret_norm[l], mix_w_out[l])
        x = x + rms_norm(mixed, mix_post_norm[l])
        x = x + 0.5 * rms_norm(swiglu(rms_norm(x, ffn2_pre_norm[l]), ffn2_w_in[l], ffn2_w_out[l]), ffn2_post_norm[l])
    return x


_drawn_inputs = setup_inputs


def setup_inputs(seed=0):
    import zlib

    import numpy as np

    out = dict(_drawn_inputs(seed))
    spreads = {}
    factors = {'ffn1_post_norm': 3.091,
     'd_skip': 17.175,
     'ssm_norm': 15.224,
     'ret_norm': 24.391,
     'ffn2_pre_norm': 4.165,
     'ffn2_post_norm': 16.487,
     'conv_b': 3.868,
     'mix_post_norm': 3.1,
     'a_log': 4.164}
    for name, (base, spread) in spreads.items():
        noise = np.random.default_rng([zlib.crc32(name.encode()), seed]).standard_normal(out[name].shape)
        drawn = base * np.exp(spread * noise) if base else spread * noise
        out[name] = __import__('jax').numpy.asarray(drawn.astype(out[name].dtype))
    for name, factor in factors.items():
        out[name] = (out[name] * factor).astype(out[name].dtype)
    return out
```

```python
from contextlib import ExitStack

import concourse.bass as bass
from concourse import mybir

F32 = mybir.dt.float32
F32R = mybir.dt.float32r
I32 = mybir.dt.int32
ACT = mybir.ActivationFunctionType
ALU = mybir.AluOpType

P = 128
L = 2
D = 1024
KD = D // P
T = 2
FF = 2816
UW = 256
UNITS = FF // UW
CELLS = 2 * UNITS
KF = FF // P
XBC = 1536
HEADS, HP, GROUPS = 16, 64, 2
RH, RK, RV = 4, 128, 256
EPS = 1e-6

RING = 4
CW = 4 * 512
FFN_CHUNKS = 2 * UNITS + KF // 2
MIX_UNITS = 11
MIX_CHUNKS = 2 * MIX_UNITS + 2 * KD // 2
LAYER_CHUNKS = 2 * FFN_CHUNKS + MIX_CHUNKS
BASE = {"f1": 0, "m": FFN_CHUNKS, "f2": FFN_CHUNKS + MIX_CHUNKS}

Z0, XS0, DT0 = 0, 1024, 2560
Q0, K0, V0, G0 = 2576, 3088, 3600, 4624
MIX_COLS = [Q0, K0, XS0, XS0 + 512, XS0 + 1024, V0, V0 + 512, Z0, Z0 + 512, G0, G0 + 512]

C_ID, C_LE, C_GT, C_DM, C_QD, C_KD, C_IF = 0, 128, 256, 384, 896, 1408, 1412
N_CONST = C_IF + 64
CUR_PRE = {"f1": 0, "m": 8, "f2": 16}
CUR_SSM, CUR_RET, CUR_CW, CUR_CB, CUR_DTB, CUR_NA, CUR_DS, N_CUR = 24, 32, 40, 88, 100, 116, 132, 148

MAGIC = 1.5 * 2.0 ** 23
ONE = 2 ** 100
INV_2PI = 15915494309189533576888376337251436203445964574046 * ONE // 10 ** 50
TWO_PI = 6.283185307179586


N_PARAM = 16 * (3 + 1 + L)


def parts(c, bits):
    out = []
    for b in bits:
        unit = ONE >> b
        n = (c + unit // 2) // unit
        out.append(n / 2 ** b)
        c -= n * unit
    return out


TURN_HIGH = parts(INV_2PI * 2 ** 15 % ONE, [7, 14, 21, 28])
TURN_LOW = parts(INV_2PI, [11, 20, 29])


class Steps:

    def __init__(self, sem, known):
        self.sem, self.known, self.names = sem, known, []

    def tick(self, name):
        assert name not in self.names, name
        self.names.append(name)
        return 1

    def at(self, name, l):
        if self.known is None:
            return l * 1 + 1
        return l * len(self.known) + self.known[name]

    def last(self, names):
        return names[0] if self.known is None else max(names, key=self.known.get)

    def result(self):
        return {n: i + 1 for i, n in enumerate(self.names)}


def by(i, step):
    return 0 if i is None else i * step


def cell_place(n):
    return (n % 2, n // 2) if n < 4 else (n // 2, n % 2)


WORK = [("rr", "act", "rr"), ("dt", "dve", "dt in")]
WORK += [(f"{a}T{t}", "act", f"{a}T{t}") for t in range(T) for a in "qk"]
WORK += [(f"xT{i}", "act", f"xT{i}") for i in range(2)]
WORK += [("sc0", "dve", "P0"), ("xT2", "act", "xT2"), ("sc1", "dve", "P1"), ("xT3", "act", "xT3")]
WORK += [("cb", "dve", "cb"), ("bT", "act", "bT"), ("dsum", "act", "ed"), ("df00", "act", "E00"),
         ("df01", "act", "E01"), ("df02", "act", "E02"),
         ("df03", "act", "E03"), ("yi00", "dve", "y00"), ("df10", "act", "E10"), ("yi01", "dve", "y01"),
         ("ss0", "act", "ss0"), ("ss1", "act", "ss1"), ("df11", "act", "E11"),
         ("rs0", "act", "rs0"), ("rs1", "act", "rs1"), ("df12", "act", "E12"), ("yi10", "dve", "y10"),
         ("yx0", "dve", "yx0"), ("df13", "act", "E13"), ("r00", "dve", "rn00"), ("r01", "dve", "rn01"),
         ("yi11", "dve", "y11"), ("yx1", "dve", "yx1"), ("r10", "dve", "rn10"), ("r11", "dve", "rn11")]
WORK += [(f"yT{j}", "dve", f"yT{j}") for j in range(4)] + [(f"rT{j}", "dve", f"rT{j}") for j in range(4)]
ORDER = [w[0] for w in WORK]
AFTER = {"rr": 3, "dt": 3, "qT0": 3, "kT0": 3, "qT1": 4, "kT1": 5, "xT0": 5, "xT1": 6, "sc0": 7, "xT2": 7, "sc1": 8,
         "xT3": 8, "cb": 10, "bT": 10, "dsum": 10, "df00": 10, "df01": 11, "df02": 11, "df03": 12,
         "yi00": 12, "df10": 12, "yi01": 13, "ss0": 13, "ss1": 13, "df11": 13, "rs0": 14, "rs1": 14,
         "df12": 14, "yi10": 15, "yx0": 15, "df13": 15, "r00": 15, "r01": 16, "yi11": 16, "yx1": 16,
         "r10": 17, "r11": 17, "yT0": 19, "yT1": 19, "yT2": 20, "yT3": 20}


def work_bank(name):
    i = ORDER.index(name)
    late = ORDER.index("yT0")
    return 4 + i % 4 if i < late else 4 + i % 2


def work_before(name):
    i = ORDER.index(name)
    for j in range(i - 1, -1, -1):
        if work_bank(ORDER[j]) == work_bank(name):
            return WORK[j]
    return None


MIX_CELL = ([("q", 0), ("k", 0), ("q", 1), ("k", 1)] + [("x", i) for i in range(4)] + [("b", 0), ("b", 1)]
            + [(a, i) for a in "vzg" for i in range(4)])
MIX_FREE = ([("dve", f"rot {a}{t}") for a, t in MIX_CELL[:4]] + [("dve", f"xr {m}") for m in range(4, 10)]
            + [("act", f"v{i}") for i in range(4)] + [("act", f"{a}{i}") for a in "zg" for i in range(4)])


def trunk(nc, a, known):
    with ExitStack() as ctx:
        def sb(name, shape, dt=F32, stack=ctx):
            return stack.enter_context(nc.sbuf_tensor(name, shape, dt))

        def sem(name):
            return ctx.enter_context(nc.semaphore(name))

        ps = ctx.enter_context(nc.psum_tensor("ps", [P, 8, 512], F32))

        raw = sb("raw", [P, RING, CW])
        w_hi = sb("w_hi", [P, RING, CW], F32R)
        w_lo = sb("w_lo", [P, RING, CW], F32R)
        x = sb("x", [P, T, D])
        u_hi = sb("u_hi", [P, KD, T * P], F32R)
        u_lo = sb("u_lo", [P, KD, T * P], F32R)
        tmp = sb("tmp", [P, 4, 512])
        tmp2 = tmp[:, :, :].rearrange("p (t a) n -> p t (a n)", t=T)
        post_w = sb("post_w", [P, D])
        const = sb("const", [P, N_CONST])
        cur = sb("cur", [P, N_CUR])
        cos = sb("cos", [P, T, 64])
        sin = sb("sin", [P, T, 64])
        par = sb("par", [P, 104])
        parw = sb("parw", [P, 96])
        bc = sb("bc", [P, 3, L, HEADS])
        dtw_raw = sb("dtw_raw", [P, L * KD * HEADS])
        dtw_hi = sb("dtw_hi", [P, KD * HEADS], F32R)
        dtw_lo = sb("dtw_lo", [P, KD * HEADS], F32R)
        na = sb("na", [P, HEADS])
        ssq = sb("ssq", [P, 8])
        ms = sb("ms", [P, 8])
        rstd = sb("rstd", [P, 8])
        neg_half = sb("neg_half", [P, 8])
        pos_i = sb("pos_i", [P, T], I32)
        pos_f = sb("pos_f", [P, T])

        with ExitStack() as ffn_only:
            h_hi = sb("h_hi", [P, KF, T * P], F32R, ffn_only)
            h_lo = sb("h_lo", [P, KF, T * P], F32R, ffn_only)
            gate = sb("gate", [P, 2, UW], F32, ffn_only)
            hh = sb("hh", [P, 2, UW], F32, ffn_only)
            turn = sb("turn", [P, 7, T * 64], F32, ffn_only)
            tmpp = sb("tmpp", [P, 10, T * 64], F32, ffn_only)
        with ExitStack() as setup_only:
            rows = sb("rows", [P, P], F32, setup_only)
            rowsw = sb("rowsw", [P, P], F32, setup_only)
        with ExitStack() as under_y:
            qT = sb("qT", [P, RH, T * P], F32, under_y)
            kT = sb("kT", [P, RH, T * P], F32, under_y)
            bcf = sb("bcf", [P, 4, T * P], F32, under_y)
            btok = sb("btok", [P, GROUPS, P], F32, under_y)
            mcb = sb("mcb", [P, T, GROUPS, P], F32, under_y)
            rrow = sb("rrow", [P, T * P], F32, under_y)
        y_hi = sb("y_hi", [P, KD, T * P], F32R)
        y_lo = sb("y_lo", [P, KD, T * P], F32R)
        ys = sb("ys", [P, T, D])
        vr = sb("vr", [P, T, D])
        kdt = sb("kdt", [P, RH, P])
        qdT = qT[:, :, P:2 * P]
        xdt = sb("xdt", [P, T, D])
        xde = post_w
        state = sb("state", [P, GROUPS, 512])
        rstate = sb("rstate", [P, RH, RV])
        uda = sb("uda", [P, 2, 4, P])
        em = sb("em", [P, 2, 4, P])
        pr = sb("pr", [P, T, RH, P])
        dts = sb("dts", [P, 10, T * HEADS])
        dtr, nab, ex, z1, z2, zq, dt, da, ed, dmx = (dts[:, i, :] for i in range(10))
        bn = sb("bn", [P, T, RH, 6])
        mv = sb("mv", [P, T, RH, 2])
        gv = sb("gv", [P, T, RH])
        grs = sb("grs", [P, T, RH])

        bcf_flat = bc[:, :, :, :].rearrange("p i l h -> p (i l h)")
        ident = const[:, C_ID:C_ID + P]
        le = const[:, C_LE:C_LE + P]
        gt = const[:, C_GT:C_GT + P]

        x_in = [sem(f"x_in{t}") for t in range(T)]
        ident_in = sem("ident_in")
        norm_rows_in = sem("norm_rows_in")
        const_in = sem("const_in")
        param_in = sem("param_in")
        raw_landed = [sem(f"raw_landed{i}") for i in range(RING)]
        hi_done = sem("hi_done")
        lo_done = sem("lo_done")
        weights_used = sem("weights_used")
        post_w_in = sem("post_w_in")
        post_w_free = sem("post_w_free")
        cell_filled = sem("cell_filled")
        gate_ready = sem("gate_ready")
        h_ready = sem("h_ready")
        hT_filled = sem("hT_filled")
        hT_hi = sem("hT_hi")
        hT_lo = sem("hT_lo")
        setup_pe = sem("setup_pe")
        setup_act = sem("setup_act")
        setup_pool = sem("setup_pool")
        stored = sem("stored")
        sp_waited = sem("sp_waited")
        pool_waited = sem("pool_waited")
        dve_waited = sem("dve_waited")
        S = {}
        for e in ("pe", "act", "dve", "pool"):
            S[e] = Steps(sem(f"{e}_steps"), known and known[e])
        PE, AC, DV, PO = S["pe"], S["act"], S["dve"], S["pool"]

        block = ctx.enter_context(nc.Block())

        def ffn_value(f, l, n, ahead=0):
            return l * (2 * CELLS) + (f == "f2") * CELLS + n + 1 + ahead

        def chunk_value(s, l, c, ahead=0):
            return l * LAYER_CHUNKS + BASE[s] + c + 1 + ahead

        def slot_of(s, c):
            return (BASE[s] + c) % RING

        def wait_steps(eng, l, needs):
            for st in S.values():
                names = [n for s_, n in needs if s_ is st]
                if names:
                    eng.wait_ge(st.sem, st.at(st.last(names), l))

        @block.sync
        def _(sp):
            for t in range(T):
                sp.dma_start(x[:, t, :], a["x"][0, t * P:(t + 1) * P, :]).then_inc(x_in[t], 16)

            def wait_apart(sem_, value):
                sp.wait_ge(sem_, value)
                sp.sem_inc(sp_waited, 1)

            def chunk(s, l, c, halves, i=None):
                slot = slot_of(s, c)
                wait_apart(lo_done, chunk_value(s, l, c) + by(i, 4))
                for h, (dst, src) in enumerate(halves):
                    sp.dma_start(dst, src).then_inc(raw_landed[slot], 16)

            def post_weights(s, l, n):
                wait_apart(post_w_free, l * 3 + n + 1)
                row = a[{"f1": "ffn1_post_norm", "m": "mix_post_norm", "f2": "ffn2_post_norm"}[s]][bass.ds(l, 1), :]
                sp.dma_start(post_w[:, :], row.broadcast_to([P, D])
                             ).then_inc(post_w_in, 16)

            def gate_up(s, l, w, c, i=None):
                u, kh = c // 2, c % 2
                dst = raw[:, slot_of(s, c), :].rearrange("p (k g n) -> p k g n", k=4, g=2)
                halves = []
                for g in range(2):
                    src = w[bass.ds(l, 1), kh * 512:(kh + 1) * 512, bass.ds(g * FF + u * UW + by(i, 2 * UW), UW)]
                    halves.append((dst[:, :, g, :], src.rearrange("a (k p) n -> p (a k) n", p=P)))
                chunk(s, l, c, halves, i)

            def down(s, l, w, first, j, i=None):
                c = first + j
                dst = raw[:, slot_of(s, c), :].rearrange("p (k n) -> p k n", k=2)
                halves = []
                for k in range(2):
                    src = w[bass.ds(l, 1), bass.ds((2 * j + k) * P + by(i, 8 * P), P), :]
                    halves.append((dst[:, k, :], src.rearrange("a p n -> (a p) n")))
                chunk(s, l, c, halves, i)

            def ffn(s, l, n):
                w1, w2 = a[f"ffn{s[1]}_w_in"], a[f"ffn{s[1]}_w_out"]
                with sp.Fori(0, 5) as i:
                    for c in range(4):
                        gate_up(s, l, w1, c, i)
                for c in range(20, 22):
                    gate_up(s, l, w1, c)
                post_weights(s, l, n)
                with sp.Fori(0, 2) as i:
                    for j in range(4):
                        down(s, l, w2, CELLS, j, i)
                for j in range(8, 11):
                    down(s, l, w2, CELLS, j)

            def mixer(l):
                for c in range(2 * MIX_UNITS):
                    u, kh = c // 2, c % 2
                    dst = raw[:, slot_of("m", c), :].rearrange("p (k n) -> p k n", k=4)
                    halves = []
                    for h in range(2):
                        r = kh * 512 + h * 256
                        src = a["mix_w_in"][bass.ds(l, 1), r:r + 256, MIX_COLS[u]:MIX_COLS[u] + 512]
                        halves.append((dst[:, 2 * h:2 * h + 2, :], src.rearrange("a (k p) n -> p (a k) n", p=P)))
                    chunk("m", l, c, halves)
                wait_apart(PE.sem, PE.at("ss1", l))
                post_weights("m", l, 1)
                for j in range(8):
                    down("m", l, a["mix_w_out"], 2 * MIX_UNITS, j)

            with sp.Fori(0, L) as l:
                ffn("f1", l, 0)
                mixer(l)
                ffn("f2", l, 2)
            for t in range(T):
                sp.wait_ge(DV.sem, DV.at(f"f2 res{t}", L - 1))
                sp.dma_start(a["out"][0, t * P:(t + 1) * P, :], x[:, t, :]).then_inc(stored, 16)
            sp.wait_ge(stored, 32)

        @block.gpsimd
        def _(pool):
            pool.memset(neg_half[:, :], -0.5).then_inc(setup_pool, 1)
            pool.wait_ge(setup_pool, 1)

            def wait_apart(sem_, value):
                pool.wait_ge(sem_, value)
                pool.sem_inc(pool_waited, 1)

            def inv_root(l, name, j, src, waits, scale, eps, n=1, srct=None, mst=None, out=None):
                for st, step in waits:
                    wait_apart(st.sem, st.at(step, l))
                srct = ssq[:, j:j + n] if srct is None else srct
                mst = ms[:, j:j + n] if mst is None else mst
                out = rstd[:, j:j + n] if out is None else out
                pool.tensor_scalar(mst, srct, scale, eps, ALU.mult, ALU.add).then_inc(PO.sem, PO.tick(name + " mean"))
                wait_apart(PO.sem, PO.at(name + " mean", l))
                pool.tensor_tensor(out, mst, neg_half[:, 0:n], ALU.pow).then_inc(PO.sem, PO.tick(name))

            def post(l, s, t):
                f = 1.0 if s == "m" else 4.0
                inv_root(l, f"{s} post{t}", t, None, [(AC, f"{s} postsq{t}")], f / D, f * EPS)

            def pre(l, s, t):
                inv_root(l, f"{s} pre{t}", 2 + t, None, [(AC, f"{s} presq{t}")], 1.0 / D, EPS)

            def op(l, name, ins):
                ins.then_inc(PO.sem, PO.tick(name))
                return name

            def mine(l, name):
                wait_apart(PO.sem, PO.at(name, l))

            def phases(l):
                mine(l, "f1 pre1")
                pool.wait_ge(param_in, N_PARAM)
                pool.wait_ge(const_in, 16)
                ang, mh, ml, af = turn[:, 3, :], turn[:, 4, :], turn[:, 5, :], turn[:, 6, :]
                keep = tmpp
                op(l, "ph pos", pool.tensor_copy(pos_f[:, :], pos_i[:, :]))
                mine(l, "ph pos")
                for t in range(T):
                    n = op(l, f"ph ang{t}", pool.tensor_scalar(
                        keep[:, 0, t * 64:(t + 1) * 64], const[:, C_IF:C_IF + 64], pos_f[:, t:t + 1], None, ALU.mult))
                mine(l, n)
                op(l, "ph h0", pool.tensor_scalar(keep[:, 1, :], keep[:, 0, :], 2.0 ** -15, MAGIC, ALU.mult, ALU.add))
                mine(l, "ph h0")
                op(l, "ph h1", pool.tensor_scalar(keep[:, 1, :], keep[:, 1, :], MAGIC, None, ALU.subtract))
                mine(l, "ph h1")
                op(l, "ph h2", pool.tensor_scalar(keep[:, 2, :], keep[:, 1, :], 2.0 ** 15, None, ALU.mult))
                mine(l, "ph h2")
                op(l, "ph l0", pool.tensor_tensor(keep[:, 0, :], keep[:, 0, :], keep[:, 2, :], ALU.subtract))
                mine(l, "ph l0")
                op(l, "ph l1", pool.tensor_scalar(keep[:, 2, :], keep[:, 0, :], MAGIC, MAGIC, ALU.add, ALU.subtract))
                mine(l, "ph l1")
                op(l, "ph f0", pool.tensor_tensor(keep[:, 0, :], keep[:, 0, :], keep[:, 2, :], ALU.subtract))
                for i, c in enumerate(TURN_HIGH):
                    n = op(l, f"ph p{i}", pool.tensor_scalar(turn[:, i, :], keep[:, 1, :], c, None, ALU.mult))
                for i, c in enumerate(TURN_LOW):
                    n = op(l, f"ph p{4 + i}", pool.tensor_scalar(turn[:, 4 + i, :], keep[:, 2, :], c, None, ALU.mult))
                mine(l, n)
                op(l, "ph r", pool.tensor_scalar(keep[:, 3:10, :], turn[:, :, :], MAGIC, MAGIC, ALU.add, ALU.subtract))
                mine(l, "ph r")
                op(l, "ph fr", pool.tensor_tensor(turn[:, :, :], turn[:, :, :], keep[:, 3:10, :], ALU.subtract))
                op(l, "ph af", pool.tensor_scalar(keep[:, 0, :], keep[:, 0, :], INV_2PI / ONE, None, ALU.mult))
                mine(l, "ph af")
                for i in range(7):
                    n = op(l, f"ph s{i}", pool.tensor_tensor(keep[:, 0, :], keep[:, 0, :], turn[:, i, :], ALU.add))
                    mine(l, n)
                op(l, "ph c0", pool.tensor_scalar(keep[:, 1, :], keep[:, 0, :], 0.25, None, ALU.add))
                mine(l, "ph c0")
                op(l, "ph r2", pool.tensor_scalar(keep[:, 2:4, :], keep[:, 0:2, :], MAGIC, MAGIC, ALU.add, ALU.subtract))
                mine(l, "ph r2")
                op(l, "phases", pool.tensor_tensor(keep[:, 0:2, :], keep[:, 0:2, :], keep[:, 2:4, :], ALU.subtract))

            def heads(ap, n, w):
                return ap.rearrange("p (h d) -> p h d", h=n) if w is None else ap

            def rotate(l, q, t, par_):
                wait_apart(DV.sem, DV.at(f"rot {q}{t}", l))
                A = tmp[:, 0, :].rearrange("p (h a d) -> p h a d", h=RH, a=2)
                B = tmp[:, 1, :].rearrange("p (h a d) -> p h a d", h=RH, a=2)
                O = tmp[:, 2 + par_, :].rearrange("p (h a d) -> p h a d", h=RH, a=2)
                if t == 1:
                    wait_apart(PE.sem, PE.at(f"{q}T0", l))
                    if q == "k":
                        mine(l, "kdt")
                op(l, f"rota {q}{t}", pool.tensor_tensor(O[:, :, 0, :], A[:, :, 0, :], B[:, :, 1, :], ALU.subtract))
                op(l, f"rot {q}{t}", pool.tensor_tensor(O[:, :, 1, :], A[:, :, 1, :], B[:, :, 0, :], ALU.add))

            def bcast_heads(tile, t, n0=0, n=HEADS):
                return tile[:, t * HEADS + n0:t * HEADS + n0 + n].unsqueeze(2).broadcast_to([P, n, HP])

            def x_heads(tile):
                return tile.rearrange("p (h d) -> p h d", d=HP)

            def decays(l, c, q, i):
                if i >= 2:
                    wait_apart(PE.sem, PE.at(f"df{(i - 2) // 4}{(i - 2) % 4}", l))
                wait_apart(DV.sem, DV.at("da", l))
                d = da[:, c * HEADS + 4 * q:c * HEADS + 4 * q + 4].unsqueeze(2).broadcast_to([P, 4, P])
                op(l, f"uda{c}{q}", pool.tensor_tensor(
                    uda[:, i % 2, :, :], le.unsqueeze(1).broadcast_to([P, 4, P]), d, ALU.mult))

            with pool.Fori(0, L) as l:
                for t in range(T):
                    pre(l, "f1", t)
                phases(l)
                for t in range(T):
                    post(l, "f1", t)
                for t in range(T):
                    pre(l, "m", t)
                rotate(l, "q", 0, 0)
                rotate(l, "k", 0, 1)
                mine(l, "rot k0")
                op(l, "kdt", pool.tensor_tensor(
                    kdt[:, :, :], tmp[:, 3, :].rearrange("p (h d) -> p h d", h=RH),
                    const[:, C_KD:C_KD + RH].unsqueeze(2).broadcast_to([P, RH, P]), ALU.mult))
                rotate(l, "q", 1, 0)
                rotate(l, "k", 1, 1)
                decays(l, 0, 0, 0)
                decays(l, 0, 1, 1)
                wait_apart(AC.sem, AC.at("xT3", l))
                op(l, "xdt0", pool.tensor_tensor(x_heads(xdt[:, 0, :]), x_heads(ys[:, 0, :]), bcast_heads(dt, 0), ALU.mult))
                decays(l, 0, 2, 2)
                decays(l, 0, 3, 3)
                wait_apart(PE.sem, PE.at("sc1", l))
                op(l, "qdT", pool.tensor_tensor(
                    qdT, qdT, const[:, C_QD:C_QD + RH * P].rearrange("p (h d) -> p h d", h=RH), ALU.mult))
                wait_apart(AC.sem, AC.at("ed", l))
                mine(l, "xdt0")
                op(l, "xde", pool.tensor_tensor(x_heads(xde[:, :]), x_heads(xdt[:, 0, :]), bcast_heads(ed, 0), ALU.mult))
                skip = cur[:, CUR_DS:CUR_DS + HEADS].unsqueeze(2).broadcast_to([P, HEADS, HP])
                op(l, "skip0", pool.tensor_tensor(x_heads(ys[:, 0, :]), x_heads(ys[:, 0, :]), skip, ALU.mult))
                decays(l, 1, 0, 4)
                op(l, "xdt1", pool.tensor_tensor(x_heads(xdt[:, 1, :]), x_heads(ys[:, 1, :]), bcast_heads(dt, 1), ALU.mult))
                decays(l, 1, 1, 5)
                mine(l, "xdt1")
                op(l, "skip1", pool.tensor_tensor(x_heads(ys[:, 1, :]), x_heads(ys[:, 1, :]), skip, ALU.mult))
                decays(l, 1, 2, 6)
                decays(l, 1, 3, 7)
                for t in range(T):
                    inv_root(l, f"gn{t}", 0, None, [(DV, f"mv{t}")], 1.0, 1e-5, RH,
                             mv[:, t, :, 1], gv[:, t, :], grs[:, t, :])
                for t in range(T):
                    inv_root(l, f"ssm rs{t}", 4 + t, None, [(AC, f"ysq{t}")], 1.0 / D, EPS)
                for t in range(T):
                    post(l, "m", t)
                for t in range(T):
                    pre(l, "f2", t)
                for t in range(T):
                    post(l, "f2", t)

        @block.scalar
        def _(act):
            act.dma_start(const[:, 0:P], a["const"][:, 0:P]).then_inc(ident_in, 16)
            names = ["ffn1_pre_norm", "mix_pre_norm", "ffn2_pre_norm", "ssm_norm", "ret_norm"]
            for i, n in enumerate(names):
                act.dma_start(rows[16 * i:16 * i + 16, :],
                              a[n].rearrange("l (k p) -> (l k) p", p=P)).then_inc(norm_rows_in, 16)
            act.dma_start(rows[80:104, :], a["conv_b"].rearrange("l (k p) -> (l k) p", p=P)).then_inc(norm_rows_in, 16)
            act.dma_start(rowsw[0:96, :], a["conv_w"].rearrange("l j (k p) -> (l j k) p", p=P)).then_inc(norm_rows_in, 16)
            act.dma_start(const[:, P:], a["const"][:, P:]).then_inc(const_in, 16)
            for i, n in enumerate(["dt_bias", "a_log", "d_skip"]):
                src = a[n].rearrange("l h -> (l h)").unsqueeze(0).broadcast_to([P, L * HEADS])
                act.dma_start(bc[:, i, :, :].rearrange("p l h -> p (l h)"), src).then_inc(param_in, 16)
            with nc.allow_non_contiguous_dma(reason="positions as a column, once"):
                act.dma_start(pos_i[:, :], a["positions"].rearrange("a (t p) -> p (a t)", p=P)).then_inc(param_in, 16)
            for l in range(L):
                act.dma_start(dtw_raw[:, l * KD * HEADS:(l + 1) * KD * HEADS].rearrange("p (k h) -> p k h", k=KD),
                              a["mix_w_in"][l, :, DT0:DT0 + HEADS].rearrange("(k p) h -> p k h", p=P)).then_inc(param_in, 16)
            act.wait_ge(setup_pe, 2)
            act.copy(par[:, :], ps[:, 0, 0:104]).then_inc(setup_act, 1)
            act.copy(parw[:, :], ps[:, 1, 0:96]).then_inc(setup_act, 1)

            def split(s, l, c, i=None):
                slot = slot_of(s, c)
                act.wait_ge(raw_landed[slot], l * (32 * LAYER_CHUNKS // RING) + by(i, 32)
                            + 32 * ((BASE[s] + c) // RING + 1))
                act.wait_ge(weights_used, chunk_value(s, l, c) + by(i, 4))
                act.activation(w_hi[:, slot, :], raw[:, slot, :], ACT.Copy).then_inc(hi_done, 1)

            def wait(st, name, l):
                act.wait_ge(st.sem, st.at(name, l))

            def postsq(l, s, t):
                b = 2 + 4 * t
                wait(PE, f"{s} acc{t}", l)
                act.activation(tmp2[:, t, :], ps[:, b:b + 2, :].rearrange("p a n -> p (a n)"), ACT.Square,
                               accum_out=ssq[:, t:t + 1]).then_inc(AC.sem, AC.tick(f"{s} postsq{t}"))

            def presq(l, s, t):
                if s == "f1":
                    act.wait_ge(x_in[t], 16)
                    wait(DV, "cur f1", l)
                else:
                    wait(DV, {"m": "f1", "f2": "m"}[s] + f" res{t}", l)
                act.activation(tmp2[:, t, :], x[:, t, :], ACT.Square,
                               accum_out=ssq[:, 2 + t:3 + t]).then_inc(AC.sem, AC.tick(f"{s} presq{t}"))

            def norm_hi(l, s, t):
                for b in range(2):
                    wait(PE, f"{s} normT{t}{b}" if b == 0 else f"{s} normT{t}", l)
                    for k in range(4):
                        kk = 4 * b + k
                        col = CUR_PRE[s] + kk
                        ins = act.activation(u_hi[:, kk, t * P:(t + 1) * P], ps[:, 4 + 2 * t + b, k * P:(k + 1) * P],
                                             ACT.Copy, scale=cur[:, col:col + 1])
                    ins.then_inc(AC.sem, AC.tick(f"{s} uhi{t}{b}"))

            def enter(l, s, before):
                if before:
                    postsq(l, before, 0)
                else:
                    wait(DV, "cur f1", l)
                split(s, l, 0)
                norm_hi(l, s, 0)
                split(s, l, 1)
                split(s, l, 2)
                if before:
                    postsq(l, before, 1)
                presq(l, s, 0)
                split(s, l, 3)
                norm_hi(l, s, 1)
                presq(l, s, 1)

            def ffn(s, l):
                def silu(m, i=None):
                    act.wait_ge(cell_filled, ffn_value(s, l, m) + by(i, 4))
                    act.wait_ge(h_ready, ffn_value(s, l, m - 2, 4) + by(i, 4))
                    t = cell_place(m)[1]
                    if m in (0, 2):
                        wait(PO, f"{s} pre{t}", l)
                    act.activation(gate[:, m % 2, :], ps[:, m % 4, 0:UW], ACT.Silu,
                                   scale=rstd[:, 2 + t:3 + t]).then_inc(gate_ready, 1)

                def h_hi_part(m, i=None):
                    u, t = cell_place(m)
                    act.wait_ge(hT_filled, ffn_value(s, l, m, 2) + by(i, 4))
                    act.activation(h_hi[:, bass.ds(2 * u + i * 4, 2), t * P:(t + 1) * P] if i is not None else
                                   h_hi[:, 2 * u:2 * u + 2, t * P:(t + 1) * P],
                                   ps[:, 4 + m % 2, 0:UW].rearrange("p (k n) -> p k n", k=2),
                                   ACT.Copy).then_inc(hT_hi, 1)

                def slot(n, i=None):
                    if 1 <= n <= CELLS:
                        silu(n - 1, i)
                    if 2 <= n <= CELLS + 1:
                        h_hi_part(n - 2, i)
                    if 4 <= n + 2 < FFN_CHUNKS:
                        split(s, l, n + 2, i)

                for n in range(6):
                    slot(n)
                with act.Fori(0, 3) as i:
                    for n in range(6, 10):
                        slot(n, i)
                for n in range(18, FFN_CHUNKS - 2):
                    slot(n)

            def mixer(l):
                def cell(m, s="m"):
                    act.wait_ge(PE.sem, PE.at(f"cell{m}", l))

                def done(name, ins):
                    ins.then_inc(AC.sem, AC.tick(name))

                def item(name):
                    wait(PE, name, l)
                    return ps[:, work_bank(name), :]

                def qk(a_, t):
                    src = item(f"{a_}T{t}").rearrange("p (h n) -> p h n", h=RH)
                    dst = (qT if a_ == "q" else kT)[:, :, t * P:(t + 1) * P]
                    done(f"{a_}T{t}", act.copy(dst, src))

                def conv_silu(m):
                    wait(DV, f"conv {m}", l)
                    cs = tmp[:, m % 2, :]
                    dst = cs if m < 8 else bcf[:, 2 * (m - 8):2 * (m - 8) + 2, :].rearrange("p f n -> p (f n)")
                    done(f"silu {m}", act.activation(dst, cs, ACT.Silu))

                def x_tok(i):
                    src = item(f"xT{i}").rearrange("p (t n) -> p t n", t=T)
                    done(f"xT{i}", act.copy(ys[:, :, i * 256:(i + 1) * 256], src))

                def decay_exp(c, q):
                    i = 4 * c + q
                    need = [(PE, f"df{c}{q}")]
                    if i >= 2:
                        j = i - 2
                        need.append((PE, f"yi{j // 4}{(j % 4) // 2}" + ("h" if j % 2 == 0 else "")))
                    wait_steps(act, l, need)
                    src = ps[:, work_bank(f"df{c}{q}"), :].rearrange("p (h n) -> p h n", h=4)
                    done(f"E{c}{q}", act.activation(em[:, i % 2, :, :], src, ACT.Exp))

                def gate_silu(a_, i):
                    m = {"z": 14, "g": 18}[a_] + i
                    cell(m)
                    if a_ == "g":
                        wait(DV, f"z{i}", l)
                    else:
                        wait(AC, "silu 9", l)
                    done(f"{a_}{i}", act.activation(tmp[:, i, :], ps[:, m % 4, :], ACT.Silu,
                                                    scale=rstd[:, 2 + i % 2:3 + i % 2]))

                def v_copy(i):
                    cell(10 + i)
                    half, t = i // 2, i % 2
                    done(f"v{i}", act.activation(vr[:, t, half * 512:(half + 1) * 512], ps[:, (10 + i) % 4, :],
                                                 ACT.Copy, scale=rstd[:, 2 + t:3 + t]))

                def y_square(t):
                    wait(DV, f"z{2 + t}", l)
                    done(f"ysq{t}", act.activation(xdt[:, t, :], ys[:, t, :], ACT.Square, accum_out=ssq[:, 4 + t:5 + t]))

                def yT(a_, j):
                    src = item(f"{a_}T{j}")
                    for kk in range(2):
                        k = 2 * j + kk
                        dst, col = (y_hi, CUR_SSM) if a_ == "y" else (u_hi, CUR_RET)
                        ins = act.activation(dst[:, k, :], src[:, kk * 256:(kk + 1) * 256], ACT.Copy,
                                             scale=cur[:, col + k:col + k + 1])
                    done(f"{a_}T{j}", ins)

                def sp_(n):
                    if 4 <= n + 2 < MIX_CHUNKS:
                        split("m", l, n + 2)

                for n in range(5):
                    sp_(n)
                    if n == 4:
                        done("rr", act.copy(rrow[:, :], item("rr")[:, 0:T * P]))
                        wait(DV, "nab", l)
                        done("na", act.activation(na[:, :], cur[:, CUR_NA:CUR_NA + HEADS], ACT.Exp))
                        done("ex", act.activation(ex, nab, ACT.Exp))
                        qk("q", 0)
                        qk("k", 0)
                sp_(5)
                qk("q", 1)
                conv_silu(4)
                sp_(6)
                qk("k", 1)
                conv_silu(5)
                x_tok(0)
                sp_(7)
                conv_silu(6)
                x_tok(1)
                sp_(8)
                conv_silu(7)
                x_tok(2)
                sp_(9)
                conv_silu(8)
                x_tok(3)
                sp_(10)
                conv_silu(9)
                sp_(11)
                v_copy(0)
                done("bT", act.copy(btok[:, :, :], item("bT")[:, 0:256].rearrange("p (g n) -> p g n", g=GROUPS)))
                wait(PE, "dsum", l)
                done("ed", act.activation(ed, ps[:, work_bank("dsum"), 0:T * HEADS], ACT.Exp))
                decay_exp(0, 0)
                sp_(12)
                v_copy(1)
                decay_exp(0, 1)
                sp_(13)
                v_copy(2)
                decay_exp(0, 2)
                decay_exp(0, 3)
                sp_(14)
                v_copy(3)
                decay_exp(1, 0)
                for g in range(GROUPS):
                    done(f"ss{g}", act.copy(state[:, g, :], item(f"ss{g}")))
                sp_(15)
                decay_exp(1, 1)
                for i in range(2):
                    done(f"rs{i}", act.copy(rstate[:, 2 * i:2 * i + 2, :].rearrange("p h n -> p (h n)"), item(f"rs{i}")))
                decay_exp(1, 2)
                sp_(16)
                decay_exp(1, 3)
                gate_silu("z", 0)
                sp_(17)
                gate_silu("z", 1)
                sp_(18)
                gate_silu("z", 2)
                gate_silu("z", 3)
                sp_(19)
                gate_silu("g", 0)
                y_square(0)
                y_square(1)
                sp_(20)
                gate_silu("g", 1)
                for j in range(2):
                    yT("y", j)
                sp_(21)
                gate_silu("g", 2)
                sp_(22)
                gate_silu("g", 3)
                for j in range(2, 4):
                    yT("y", j)
                for j in range(2):
                    yT("r", j)
                sp_(23)
                for j in range(2, 4):
                    yT("r", j)
                for n in range(24, MIX_CHUNKS - 2):
                    sp_(n)

            with act.Fori(0, L) as l:
                enter(l, "f1", None)
                ffn("f1", l)
                wait(PO, "phases", l)
                act.activation(sin[:, :, :], tmpp[:, 0, :].rearrange("p (t n) -> p t n", t=T), ACT.Sin,
                               scale=TWO_PI).then_inc(AC.sem, AC.tick("sin"))
                act.activation(cos[:, :, :], tmpp[:, 1, :].rearrange("p (t n) -> p t n", t=T), ACT.Sin,
                               scale=TWO_PI).then_inc(AC.sem, AC.tick("cos"))
                enter(l, "m", "f1")
                mixer(l)
                enter(l, "f2", "m")
                ffn("f2", l)
                for t in range(T):
                    postsq(l, "f2", t)

        @block.vector
        def _(dve):
            dve.sem_inc(lo_done, RING)
            dve.sem_inc(h_ready, 4)
            dve.sem_inc(hT_lo, 2)
            dve.sem_inc(post_w_free, 1)
            dve.wait_ge(setup_act, 2)

            def split(s, l, c, i=None):
                slot = slot_of(s, c)
                dve.wait_ge(hi_done, chunk_value(s, l, c) + by(i, 4))
                dve.tensor_tensor(w_lo[:, slot, :], raw[:, slot, :], w_hi[:, slot, :].bitcast(F32),
                                  ALU.subtract).then_inc(lo_done, 1)

            def wait(st, name, l):
                dve.wait_ge(st.sem, st.at(name, l))

            def done(name, ins):
                ins.then_inc(DV.sem, DV.tick(name))

            def chain(name, l, ins):
                ins.then_inc(DV.sem, DV.tick(name))
                dve.wait_ge(DV.sem, DV.at(name, l))

            def residual(l, s, n, t):
                b = 2 + 4 * t
                wait(PO, f"{s} post{t}", l)
                dve.wait_ge(post_w_in, l * 48 + 16 * (n + 1))
                chain(f"{s} scaled{t}", l, dve.scalar_tensor_tensor(
                    tmp2[:, t, :], ps[:, b:b + 2, :].rearrange("p a n -> p (a n)"), rstd[:, t:t + 1], post_w[:, :],
                    ALU.mult, ALU.mult))
                if t == 1:
                    dve.sem_inc(post_w_free, 1)
                chain(f"{s} res{t}", l, dve.tensor_tensor(x[:, t, :], x[:, t, :], tmp2[:, t, :], ALU.add))

            def norm_lo(l, s, t):
                for b in range(2):
                    wait(AC, f"{s} uhi{t}{b}", l)
                    for k in range(4):
                        kk = 4 * b + k
                        col = CUR_PRE[s] + kk
                        ins = dve.scalar_tensor_tensor(
                            u_lo[:, kk, t * P:(t + 1) * P], ps[:, 4 + 2 * t + b, k * P:(k + 1) * P],
                            cur[:, col:col + 1], u_hi[:, kk, t * P:(t + 1) * P].bitcast(F32), ALU.mult, ALU.subtract)
                    done(f"{s} ulo{t}{b}", ins)

            def enter(l, s, before, n):
                if before:
                    residual(l, before, n, 0)
                split(s, l, 0)
                norm_lo(l, s, 0)
                split(s, l, 1)
                split(s, l, 2)
                if before:
                    residual(l, before, n, 1)
                split(s, l, 3)
                norm_lo(l, s, 1)

            def ffn(s, l):
                def product(m, i=None):
                    dve.wait_ge(gate_ready, ffn_value(s, l, m) + by(i, 4))
                    dve.wait_ge(hT_filled, ffn_value(s, l, m - 2, 2) + by(i, 4))
                    t = cell_place(m)[1]
                    if m in (0, 2):
                        wait(PO, f"{s} pre{t}", l)
                    dve.scalar_tensor_tensor(hh[:, m % 2, :], ps[:, m % 4, UW:2 * UW], rstd[:, 2 + t:3 + t],
                                             gate[:, m % 2, :], ALU.mult, ALU.mult).then_inc(h_ready, 1)

                def h_lo_part(m, i=None):
                    u, t = cell_place(m)
                    dve.wait_ge(hT_hi, ffn_value(s, l, m) + by(i, 4))
                    k = slice(2 * u, 2 * u + 2) if i is None else bass.ds(2 * u + i * 4, 2)
                    dve.tensor_tensor(h_lo[:, k, t * P:(t + 1) * P],
                                      ps[:, 4 + m % 2, 0:UW].rearrange("p (k n) -> p k n", k=2),
                                      h_hi[:, k, t * P:(t + 1) * P].bitcast(F32), ALU.subtract).then_inc(hT_lo, 1)

                def slot(n, i=None):
                    if 1 <= n <= CELLS:
                        product(n - 1, i)
                    if 2 <= n <= CELLS + 1:
                        h_lo_part(n - 2, i)
                    if 4 <= n + 2 < FFN_CHUNKS:
                        split(s, l, n + 2, i)

                for n in range(6):
                    slot(n)
                with dve.Fori(0, 3) as i:
                    for n in range(6, 10):
                        slot(n, i)
                for n in range(18, FFN_CHUNKS - 2):
                    slot(n)

            def mixer(l):
                def item(name):
                    wait(PE, name, l)
                    return ps[:, work_bank(name), :]

                def cell(m):
                    wait(PE, f"cell{m}", l)
                    return ps[:, m % 4, :]

                def rotate(a_, t, m, before):
                    src = cell(m).rearrange("p (h n) -> p h n", n=64)
                    if before:
                        wait(PO, f"rot {before}", l)
                    if not before:
                        wait(PO, "m pre1", l)
                    wait(AC, "cos", l)
                    r = rstd[:, 2 + t:3 + t]
                    done(f"rotc {a_}{t}", dve.scalar_tensor_tensor(
                        tmp[:, 0, :].rearrange("p (h n) -> p h n", n=64), src, r,
                        cos[:, t, :].unsqueeze(1).broadcast_to([P, 2 * RH, 64]), ALU.mult, ALU.mult))
                    done(f"rot {a_}{t}", dve.scalar_tensor_tensor(
                        tmp[:, 1, :].rearrange("p (h n) -> p h n", n=64), src, r,
                        sin[:, t, :].unsqueeze(1).broadcast_to([P, 2 * RH, 64]), ALU.mult, ALU.mult))

                def softplus():
                    b = item("dt")
                    for t in range(T):
                        o = slice(t * HEADS, (t + 1) * HEADS)
                        ins = dve.scalar_tensor_tensor(dtr[:, o], b[:, o], rstd[:, 2 + t:3 + t],
                                                       cur[:, CUR_DTB:CUR_DTB + HEADS], ALU.mult, ALU.add)
                    chain("dt in", l, ins)
                    chain("nab", l, dve.scalar_tensor_tensor(nab, dtr, -1.0, dtr, ALU.mult, ALU.min))

                def softplus2():
                    wait(AC, "ex", l)
                    chain("dmx", l, dve.tensor_scalar(dmx, dtr, 0.0, None, ALU.max))
                    chain("sp0", l, dve.tensor_scalar(z1, ex, 2.0, None, ALU.add))
                    chain("sp1", l, dve.reciprocal(z1, z1))
                    chain("sp2", l, dve.tensor_tensor(z1, z1, ex, ALU.mult))
                    chain("sp3", l, dve.tensor_tensor(z2, z1, z1, ALU.mult))
                    chain("sp4", l, dve.tensor_scalar(zq, z2, 1.0 / 15, None, ALU.mult))
                    for n in (13, 11, 9, 7, 5, 3):
                        chain(f"zq{n}", l, dve.scalar_tensor_tensor(zq, zq, 1.0 / n, z2, ALU.add, ALU.mult))
                    chain("sp5", l, dve.scalar_tensor_tensor(zq, zq, 1.0, z1, ALU.add, ALU.mult))
                    chain("dt", l, dve.scalar_tensor_tensor(dt, zq, 2.0, dmx, ALU.mult, ALU.add))
                    chain("da", l, dve.scalar_tensor_tensor(
                        da.rearrange("p (t h) -> p t h", t=T), dt.rearrange("p (t h) -> p t h", t=T), -1.0,
                        na[:, :].unsqueeze(1).broadcast_to([P, T, HEADS]), ALU.mult, ALU.mult))

                def conv(m, free):
                    wait_steps(dve, l, [(PE, f"cell{m}")] + free)
                    src = tmp[:, 2 + m % 2, :]
                    chain(f"xr {m}", l, dve.tensor_tensor(
                        src.rearrange("p (f n) -> p f n", f=2), ps[:, m % 4, :].rearrange("p (f n) -> p f n", f=2),
                        rrow[:, :].unsqueeze(1).broadcast_to([P, 2, T * P]), ALU.mult))
                    for tap in range(3, -1, -1):
                        for f in range(2):
                            ft = 2 * (m - 4) + f
                            w = cur[:, CUR_CW + tap * 12 + ft:CUR_CW + tap * 12 + ft + 1]
                            o = tmp[:, m % 2, f * 256:(f + 1) * 256]
                            s_ = src[:, f * 256:(f + 1) * 256]
                            sh = 3 - tap
                            if tap == 3:
                                ins = dve.tensor_scalar(o, s_, w, cur[:, CUR_CB + ft:CUR_CB + ft + 1], ALU.mult, ALU.add)
                            else:
                                ins = dve.scalar_tensor_tensor(o[:, sh:256], s_[:, 0:256 - sh], w, o[:, sh:256],
                                                               ALU.mult, ALU.add)
                            if tap and f == 0:
                                done(f"conv {m} {tap}{f}", ins)
                            elif tap:
                                chain(f"conv {m} {tap}{f}", l, ins)
                    done(f"conv {m}", ins)

                def scores(c):
                    done(f"P{c}", dve.tensor_tensor(
                        pr[:, c, :, :], item(f"sc{c}").rearrange("p (h n) -> p h n", h=RH),
                        const[:, C_DM:C_DM + RH * P].rearrange("p (h n) -> p h n", h=RH), ALU.mult))

                def mix(c, q):
                    i = 4 * c + q
                    wait(AC, f"E{c}{q}", l)
                    done(f"M{c}{q}", dve.tensor_tensor(
                        em[:, i % 2, :, :], em[:, i % 2, :, :],
                        mcb[:, c, q // 2, :].unsqueeze(1).broadcast_to([P, 4, P]), ALU.mult))

                def add_y(c, g):
                    o = ys[:, c, g * 512:(g + 1) * 512]
                    b = item(f"yi{c}{g}")
                    wait(PO, f"skip{c}", l)
                    chain(f"y{c}{g}", l, dve.tensor_tensor(o, b, o, ALU.add))

                def add_state(g):
                    o = ys[:, 1, g * 512:(g + 1) * 512]
                    e = ed[:, HEADS + 8 * g:HEADS + 8 * g + 8].unsqueeze(2).broadcast_to([P, 8, HP])
                    chain(f"yx{g}", l, dve.tensor_tensor(
                        xdt[:, 0, g * 512:(g + 1) * 512].rearrange("p (h d) -> p h d", h=8),
                        item(f"yx{g}").rearrange("p (h d) -> p h d", h=8), e, ALU.mult))
                    chain(f"ya{g}", l, dve.tensor_tensor(o, o, xdt[:, 0, g * 512:(g + 1) * 512], ALU.add))

                def moments(t, half):
                    b = item(f"r{t}{half}")
                    for h in range(2):
                        n = f"bn{t}{2 * half + h}"
                        done(n, dve.bn_stats(bn[:, t, 2 * half + h, :], b[:, h * RV:(h + 1) * RV]))
                    wait(DV, n, l)
                    dve.sem_inc(dve_waited, 1)
                    for h in range(2):
                        n = f"mv{t}{2 * half + h}" if (half, h) != (1, 1) else f"mv{t}"
                        done(n, dve.bn_aggr(mv[:, t, 2 * half + h, :], bn[:, t, 2 * half + h, :]))

                def group_norm(t):
                    wait(PO, f"gn{t}", l)
                    for half in range(2):
                        for h in range(2):
                            hd = 2 * half + h
                            ins = dve.tensor_scalar(vr[:, t, hd * RV:(hd + 1) * RV],
                                                    ps[:, work_bank(f"r{t}{half}"), h * RV:(h + 1) * RV],
                                                    mv[:, t, hd, 0:1], grs[:, t, hd:hd + 1], ALU.subtract, ALU.mult)
                        done(f"rn{t}{half}", ins)

                def gated(a_, i):
                    t, half = i % 2, i // 2
                    o = (ys if a_ == "z" else vr)[:, t, half * 512:(half + 1) * 512]
                    wait(AC, f"{a_}{i}", l)
                    if a_ == "g":
                        wait(DV, f"rn{t}{half}", l)
                    done(f"{a_}{i}", dve.tensor_tensor(o, o, tmp[:, i, :], ALU.mult))

                def ssm_norm(t):
                    wait(PO, f"ssm rs{t}", l)
                    done(f"yn{t}", dve.tensor_scalar(ys[:, t, :], ys[:, t, :], rstd[:, 4 + t:5 + t], None, ALU.mult))

                def yT(a_, j):
                    wait(AC, f"{a_}T{j}", l)
                    b = ps[:, work_bank(f"{a_}T{j}"), :]
                    for kk in range(2):
                        k = 2 * j + kk
                        hi, lo, col = (y_hi, y_lo, CUR_SSM) if a_ == "y" else (u_hi, u_lo, CUR_RET)
                        ins = dve.scalar_tensor_tensor(lo[:, k, :], b[:, kk * 256:(kk + 1) * 256],
                                                       cur[:, col + k:col + k + 1], hi[:, k, :].bitcast(F32),
                                                       ALU.mult, ALU.subtract)
                    done(f"{a_}T{j}", ins)

                def sp_(n):
                    if 4 <= n + 2 < MIX_CHUNKS:
                        split("m", l, n + 2)

                dve.wait_ge(param_in, N_PARAM)
                chain("dtw hi", l, dve.tensor_copy(dtw_hi[:, :], dtw_raw[:, bass.ds(l * (KD * HEADS), KD * HEADS)]))
                done("dtw lo", dve.tensor_tensor(dtw_lo[:, :], dtw_raw[:, bass.ds(l * (KD * HEADS), KD * HEADS)],
                                                 dtw_hi[:, :].bitcast(F32), ALU.subtract))
                sp_(0)
                rotate("q", 0, 0, None)
                sp_(1)
                rotate("k", 0, 1, "q0")
                sp_(2)
                rotate("q", 1, 2, "k0")
                sp_(3)
                rotate("k", 1, 3, "q1")
                softplus()
                sp_(4)
                softplus2()
                conv(4, [(PO, "rot k1"), (PE, "qT1"), (AC, "rr")])
                sp_(5)
                conv(5, [(PE, "kT1")])
                sp_(6)
                conv(6, [(PE, "xT0")])
                sp_(7)
                scores(0)
                conv(7, [(PE, "xT1")])
                sp_(8)
                conv(8, [(PE, "xT2")])
                sp_(9)
                scores(1)
                conv(9, [(PE, "xT3")])
                sp_(10)
                sp_(11)
                done("cb", dve.tensor_tensor(
                    mcb[:, :, :, :].rearrange("p c g n -> p (c g) n"), item("cb").rearrange("p (a n) -> p a n", a=4),
                    le.unsqueeze(1).broadcast_to([P, 4, P]), ALU.mult))
                wait(DV, "cb", l)
                mix(0, 0)
                sp_(12)
                mix(0, 1)
                sp_(13)
                mix(0, 2)
                add_y(0, 0)
                mix(0, 3)
                sp_(14)
                mix(1, 0)
                add_y(0, 1)
                sp_(15)
                mix(1, 1)
                gated_z = lambda i: gated("z", i)
                add_y(1, 0)
                mix(1, 2)
                sp_(16)
                add_state(0)
                mix(1, 3)
                moments(0, 0)
                moments(0, 1)
                gated_z(0)
                add_y(1, 1)
                sp_(17)
                add_state(1)
                group_norm(0)
                gated_z(1)
                sp_(18)
                gated_z(2)
                moments(1, 0)
                moments(1, 1)
                gated_z(3)
                sp_(19)
                group_norm(1)
                gated("g", 0)
                ssm_norm(0)
                ssm_norm(1)
                sp_(20)
                gated("g", 1)
                yT("y", 0)
                yT("y", 1)
                sp_(21)
                gated("g", 2)
                sp_(22)
                gated("g", 3)
                yT("y", 2)
                yT("y", 3)
                yT("r", 0)
                yT("r", 1)
                sp_(23)
                yT("r", 2)
                yT("r", 3)
                for n in range(24, MIX_CHUNKS - 2):
                    sp_(n)

            with dve.Fori(0, L) as l:
                done("cur f1", dve.tensor_copy(cur[:, 0:8], par[:, bass.ds(l * 8, 8)]))
                enter(l, "f1", None, None)
                for i in range(1, 5):
                    done(f"cur{i}", dve.tensor_copy(cur[:, 8 * i:8 * i + 8], par[:, bass.ds(l * 8 + 16 * i, 8)]))
                done("cur cw", dve.tensor_copy(cur[:, CUR_CW:CUR_CW + 48], parw[:, bass.ds(l * 48, 48)]))
                done("cur cb", dve.tensor_copy(cur[:, CUR_CB:CUR_CB + 12], par[:, bass.ds(l * 12 + 80, 12)]))
                dve.wait_ge(param_in, N_PARAM)
                for i in range(2):
                    done(f"cur b{i}", dve.tensor_copy(cur[:, CUR_DTB + 16 * i:CUR_DTB + 16 * i + 16],
                                                      bcf_flat[:, bass.ds(l * 16 + 32 * i, 16)]))
                chain("cur", l, dve.tensor_copy(cur[:, CUR_DS:CUR_DS + 16], bcf_flat[:, bass.ds(l * 16 + 64, 16)]))
                ffn("f1", l)
                enter(l, "m", "f1", 0)
                mixer(l)
                enter(l, "f2", "m", 1)
                ffn("f2", l)
                for t in range(T):
                    residual(l, "f2", 2, t)

        @block.tensor
        def _(pe):
            pe.sem_inc(weights_used, RING - 1)
            pe.sem_inc(hT_filled, 2)
            pe.wait_ge(ident_in, 16)
            pe.wait_ge(norm_rows_in, 16 * 7)
            pe.transpose(ps[:, 0, 0:104], rows[0:104, :], ident[0:104, 0:104]).then_inc(setup_pe, 1)
            pe.transpose(ps[:, 1, 0:96], rowsw[0:96, :], ident[0:96, 0:96]).then_inc(setup_pe, 1)
            pe.wait_ge(setup_act, 2)

            def wait(st, name, l):
                pe.wait_ge(st.sem, st.at(name, l))

            def three(out, s_hi, s_lo, m_hi, m_lo, start, stop, release=False):
                first = pe.matmul(out, s_hi, m_hi, start=start, stop=False)
                if release:
                    first.then_inc(weights_used, 1)
                pe.matmul(out, s_hi, m_lo, start=False, stop=False)
                return pe.matmul(out, s_lo, m_hi, start=False, stop=stop)

            def norm_transpose(l, s, t):
                if s == "f1":
                    pe.wait_ge(x_in[t], 16)
                    wait(DV, "cur f1", l)
                else:
                    wait(DV, {"m": "f1", "f2": "m"}[s] + f" res{t}", l)
                for b in range(2):
                    for k in range(4):
                        kk = 4 * b + k
                        ins = pe.transpose(ps[:, 4 + 2 * t + b, k * P:(k + 1) * P], x[:, t, kk * P:(kk + 1) * P], ident)
                    ins.then_inc(PE.sem, PE.tick(f"{s} normT{t}{b}" if b == 0 else f"{s} normT{t}"))

            def after_unit(n):
                return n == 0 or n == 3 or (n >= 4 and n % 2 == 0)

            def cell(s, l, n, i=None):
                u, t = cell_place(n)
                c0, bank, last = 2 * u, n % 4, t == 1
                for kh in range(2):
                    if n == 1 and kh == 1:
                        norm_transpose(l, s, 1)
                    c = c0 + kh
                    slot = slot_of(s, c)
                    pe.wait_ge(lo_done, chunk_value(s, l, c, RING) + by(i, 4))
                    for k in range(4):
                        kk = 4 * kh + k
                        cols = slice(k * 512, (k + 1) * 512)
                        ts = slice(t * P, (t + 1) * P)
                        ins = three(ps[:, bank, :], u_hi[:, kk, ts], u_lo[:, kk, ts], w_hi[:, slot, cols],
                                    w_lo[:, slot, cols], kk == 0, kk == KD - 1, after_unit(n) and kk == 0)
                    if last and kh == 0:
                        ins.then_inc(weights_used, 1)
                return ins

            def down(s, l, first, j, tts, stat, last, nj):
                c = first + j
                slot = slot_of(s, c)
                pe.wait_ge(lo_done, chunk_value(s, l, c, RING))
                for k in range(2):
                    kt = 2 * j + k
                    hi, lo, kk = stat(kt)
                    for t in tts:
                        ts = slice(t * P, (t + 1) * P)
                        st, en = kt == 0, kt == 2 * nj - 1
                        for n in range(2):
                            out = ps[:, 2 + 4 * t + n, :]
                            cols = slice(k * D + n * 512, k * D + (n + 1) * 512)
                            ins = three(out, hi[:, kk, ts], lo[:, kk, ts], w_hi[:, slot, cols],
                                        w_lo[:, slot, cols], st, en, kt == 0 and t == 0 and n == 0)
                if last and j < nj - 1:
                    ins.then_inc(weights_used, 1)
                return ins

            def down_tail(s, l, first, nj, stat, then):
                for t in range(T):
                    for j in range(nj - RING, nj):
                        if t == 1 and j == nj - 2 and then:
                            norm_transpose(l, then, 0)
                        ins = down(s, l, first, j, [t], stat, t == 1, nj)
                    ins.then_inc(PE.sem, PE.tick(f"{s} acc{t}"))

            def ffn(s, l, then):
                def one(n, i=None):
                    u, t = cell_place(n)
                    pe.wait_ge(h_ready, ffn_value(s, l, n - 4, 4) + by(i, 4))
                    if n in (0, 2):
                        wait(DV, f"{s} ulo{t}1", l)
                    ins = cell(s, l, n, i)
                    ins.then_inc(cell_filled, 1)

                def turn_h(m, i=None):
                    pe.wait_ge(h_ready, ffn_value(s, l, m, 4) + by(i, 4))
                    pe.wait_ge(hT_lo, ffn_value(s, l, m - 2, 2) + by(i, 4))
                    for k in range(2):
                        ins = pe.transpose(ps[:, 4 + m % 2, k * P:(k + 1) * P], hh[:, m % 2, k * P:(k + 1) * P], ident)
                    ins.then_inc(hT_filled, 1)

                one(0)
                one(1)
                turn_h(0)
                for n in (2, 3):
                    one(n)
                    turn_h(n - 1)
                with pe.Fori(0, 4) as i:
                    for n in range(4, 8):
                        one(n, i)
                        turn_h(n - 1, i)
                for n in (20, 21):
                    one(n)
                    turn_h(n - 1)

                def stat(kt):
                    return h_hi, h_lo, kt

                nj = KF // 2
                for j in range(nj - RING):
                    m = {0: 2, 1: 3}.get(j, 2 * j + 1)
                    pe.wait_ge(hT_lo, ffn_value(s, l, m, 2))
                    down(s, l, CELLS, j, range(T), stat, True, nj)
                    if j == 0:
                        turn_h(21)
                pe.wait_ge(hT_lo, ffn_value(s, l, CELLS - 1, 2))
                down_tail(s, l, CELLS, nj, stat, then)

            def mixer(l):
                def work(name):
                    before = work_before(name)
                    need = [(S[before[1]], before[2])] if before else []
                    b = ps[:, work_bank(name), :]
                    kind, last = name[:2], None
                    if name == "rr":
                        wait_steps(pe, l, need + [(PO, "m pre1")])
                        for t in range(T):
                            last = pe.matmul(b[:, t * P:(t + 1) * P], rstd[:, 2 + t:3 + t].broadcast_to([P, P]), ident,
                                             start=True, stop=True)
                    elif name == "dt":
                        wait_steps(pe, l, need + [(DV, "dtw lo")])
                        for t in range(T):
                            ts = slice(t * P, (t + 1) * P)
                            for k in range(KD):
                                cols = slice(k * HEADS, (k + 1) * HEADS)
                                last = three(b[:, t * HEADS:(t + 1) * HEADS], u_hi[:, k, ts], u_lo[:, k, ts],
                                             dtw_hi[:, cols], dtw_lo[:, cols], k == 0, k == KD - 1)
                    elif kind in ("qT", "kT"):
                        t = int(name[2])
                        wait_steps(pe, l, need + [(PO, f"rot {name[0]}{t}")])
                        for h in range(RH):
                            last = pe.transpose(b[:, h * P:(h + 1) * P],
                                                tmp[:, 2 + "qk".index(name[0]), h * P:(h + 1) * P], ident)
                    elif kind == "xT":
                        m = 4 + int(name[2])
                        wait_steps(pe, l, need + [(AC, f"silu {m}")])
                        for t in range(T):
                            for f in range(2):
                                last = pe.transpose(b[:, (2 * t + f) * P:(2 * t + f + 1) * P],
                                                    tmp[:, m % 2, f * 256 + t * P:f * 256 + (t + 1) * P], ident)
                    elif kind == "sc":
                        c = int(name[2])
                        cs = slice(c * P, (c + 1) * P)
                        wait_steps(pe, l, need + [(AC, f"qT{c}"), (AC, f"kT{c}")])
                        for h in range(RH):
                            last = pe.matmul(b[:, h * P:(h + 1) * P], kT[:, h, cs], qT[:, h, cs], start=True, stop=True)
                    elif name == "cb":
                        wait_steps(pe, l, need + [(AC, "silu 9")])
                        for c in range(T):
                            cs = slice(c * P, (c + 1) * P)
                            for g in range(GROUPS):
                                o = (c * GROUPS + g) * P
                                last = pe.matmul(b[:, o:o + P], bcf[:, g, cs], bcf[:, GROUPS + g, cs], start=True, stop=True)
                    elif name == "bT":
                        wait_steps(pe, l, need + [(AC, "silu 8")])
                        for g in range(GROUPS):
                            last = pe.transpose(b[:, g * P:(g + 1) * P], bcf[:, g, 0:P], ident)
                    elif name == "dsum":
                        wait_steps(pe, l, need + [(DV, "da")])
                        pe.matmul(b[:, 0:HEADS], gt, da[:, 0:HEADS], start=True, stop=True)
                        last = pe.matmul(b[:, HEADS:2 * HEADS], le, da[:, HEADS:2 * HEADS], start=True, stop=True)
                    elif kind == "df":
                        c, q = int(name[2]), int(name[3])
                        wait_steps(pe, l, need + [(PO, f"uda{c}{q}")])
                        last = pe.matmul(b, gt, uda[:, (4 * c + q) % 2, :, :].rearrange("p h n -> p (h n)"),
                                         start=True, stop=True)
                    elif kind == "yi":
                        c, g = int(name[2]), int(name[3])
                        for q in range(2):
                            qq = 2 * g + q
                            own = [(DV, f"M{c}{qq}")]
                            wait_steps(pe, l, own if q else need + own + [(PO, f"xdt{c}")])
                            for h in range(4):
                                o = (4 * q + h) * HP
                                hd = g * 512 + o
                                last = pe.matmul(b[:, o:o + HP], em[:, qq % 2, h, :], xdt[:, c, hd:hd + HP],
                                                 start=True, stop=True)
                            if q == 0:
                                last.then_inc(PE.sem, PE.tick(name + "h"))
                    elif kind == "ss":
                        g = int(name[2])
                        wait_steps(pe, l, need + [(AC, "bT"), (PO, "xde")])
                        last = pe.matmul(b, btok[:, g, :], xde[:, g * 512:(g + 1) * 512], start=True, stop=True)
                    elif kind == "yx":
                        g = int(name[2])
                        wait_steps(pe, l, need + [(AC, f"ss{g}")])
                        last = pe.matmul(b, bcf[:, GROUPS + g, P:2 * P], state[:, g, :], start=True, stop=True)
                    elif kind == "rs":
                        i = int(name[2])
                        wait_steps(pe, l, need + [(PO, "kdt"), (AC, f"v{2 * i}")])
                        for h in range(2):
                            hd = 2 * i + h
                            last = pe.matmul(b[:, h * RV:(h + 1) * RV], kdt[:, hd, :], vr[:, 0, hd * RV:(hd + 1) * RV],
                                             start=True, stop=True)
                    elif kind in ("r0", "r1"):
                        c, half = int(name[1]), int(name[2])
                        own = [(DV, f"P{c}"), (AC, f"v{2 * half + c}")]
                        if c == 1:
                            own += [(PO, "qdT"), (AC, f"rs{half}")]
                        wait_steps(pe, l, need + own)
                        for h in range(2):
                            hd = 2 * half + h
                            o = b[:, h * RV:(h + 1) * RV]
                            last = pe.matmul(o, pr[:, c, hd, :], vr[:, c, hd * RV:(hd + 1) * RV], start=True, stop=c == 0)
                            if c == 1:
                                last = pe.matmul(o, qdT[:, hd, :], rstate[:, hd, :], start=False, stop=True)
                    elif kind in ("yT", "rT"):
                        j = int(name[2])
                        src = ys if kind == "yT" else vr
                        wait_steps(pe, l, need + [(DV, f"yn{t}" if kind == "yT" else f"g{2 * (j // 2) + t}")
                                                  for t in range(T)])
                        for kk in range(2):
                            for t in range(T):
                                k = 2 * j + kk
                                o = (2 * kk + t) * P
                                last = pe.transpose(b[:, o:o + P], src[:, t, k * P:(k + 1) * P], ident)
                    last.then_inc(PE.sem, PE.tick(name))

                for m in range(CELLS):
                    kind, i = MIX_CELL[m]
                    if m in (0, 2):
                        wait(DV, f"m ulo{m // 2}1", l)
                    if m >= 4:
                        st, name = MIX_FREE[m - 4]
                        wait(S[st], name, l)
                    u, t = cell_place(m)
                    if kind in "xb":
                        half = m % 2
                        pe.wait_ge(lo_done, chunk_value("m", l, 2 * u + 1, RING))
                        for f in range(2):
                            for k in range(KD):
                                slot = slot_of("m", 2 * u + k // 4)
                                o = (k % 4) * 512 + (2 * half + f) * P
                                cols = slice(o, o + P)
                                ins = three(ps[:, m % 4, f * 256:(f + 1) * 256], w_hi[:, slot, cols], w_lo[:, slot, cols],
                                            u_hi[:, k, :], u_lo[:, k, :], k == 0, k == KD - 1,
                                            after_unit(m) and f == 0 and k == 0)
                                if half and f and k == 3:
                                    ins.then_inc(weights_used, 1)
                    else:
                        ins = cell("m", l, m)
                    ins.then_inc(PE.sem, PE.tick(f"cell{m}"))
                    for name in ORDER:
                        if AFTER.get(name) == m:
                            work(name)

                def stat(kt):
                    return (y_hi, y_lo, kt) if kt < KD else (u_hi, u_lo, kt - KD)

                wait(AC, "g3", l)
                for j in range(4):
                    wait(DV, f"yT{j}", l)
                    down("m", l, CELLS, j, range(T), stat, True, 8)
                    if j < 2:
                        for i in range(2):
                            work(f"rT{2 * j + i}")
                wait(DV, "rT3", l)
                down_tail("m", l, CELLS, 8, stat, "f2")

            with pe.Fori(0, L) as l:
                norm_transpose(l, "f1", 0)
                ffn("f1", l, "m")
                mixer(l)
                ffn("f2", l, None)

    return {e: s.result() for e, s in S.items()}


NAMES = ["x", "positions", "ffn1_pre_norm", "ffn1_w_in", "ffn1_w_out", "ffn1_post_norm", "mix_pre_norm",
         "mix_w_in", "conv_w", "conv_b", "dt_bias", "a_log", "d_skip", "ssm_norm", "ret_norm", "mix_w_out",
         "mix_post_norm", "ffn2_pre_norm", "ffn2_w_in", "ffn2_w_out", "ffn2_post_norm"]


def constants(np):
    c = np.zeros((P, N_CONST), np.float32)
    row, col = np.arange(P)[:, None], np.arange(P)[None, :]
    c[:, C_ID:C_ID + P] = row == col
    c[:, C_LE:C_LE + P] = row <= col
    c[:, C_GT:C_GT + P] = row > col
    scale = RK ** -0.5
    for h in range(RH):
        lg = np.log(1.0 - 2.0 ** (-5.0 - h))
        c[:, C_DM + h * P:C_DM + (h + 1) * P] = np.where(row <= col, np.exp((col - row) * lg), 0.0) * scale
        c[:, C_QD + h * P:C_QD + (h + 1) * P] = np.exp((col + 1.0) * lg)
        c[:, C_KD + h] = np.exp((P - 1.0 - row[:, 0]) * lg) * scale
    c[:, C_IF:C_IF + 64] = np.float32(10000.0) ** (-np.arange(64, dtype=np.float32) / np.float32(64))
    return c


def kernel(**inputs):
    import numpy as np
    import concourse.bacc as bacc
    from concourse.bass_utils import run_bass_kernel_spmd

    def build(known):
        nc = bacc.Bacc("TRN2", target_bir_lowering=False, num_devices=1)
        aps = {}
        for n, v in arrays.items():
            aps[n] = nc.dram_tensor(f"in_{n}", v.shape, mybir.dt.from_np(v.dtype), kind="ExternalInput").ap()
        aps["out"] = nc.dram_tensor("out", arrays["x"].shape, F32, kind="ExternalOutput").ap()
        return nc, trunk(nc, aps, known)

    arrays = {n: np.ascontiguousarray(inputs[n]) for n in NAMES}
    arrays["const"] = constants(np)
    _, steps = build(None)
    nc, _ = build(steps)
    r = run_bass_kernel_spmd(nc, [{f"in_{n}": v for n, v in arrays.items()}], core_ids=[0])
    return r.results[0]["out"]
```

```python
from contextlib import ExitStack

import concourse.bass as bass
from concourse import mybir

F32 = mybir.dt.float32
F32R = mybir.dt.float32r
I32 = mybir.dt.int32
ACT = mybir.ActivationFunctionType
ALU = mybir.AluOpType

P = 128
L = 2
D = 1024
KD = D // P
T = 2
FF = 2816
UW = 256
UNITS = FF // UW
CELLS = 2 * UNITS
TM_CELLS = 4
KF = FF // P
HEADS, HP, GROUPS = 16, 64, 2
RH, RK, RV = 4, 128, 256
EPS = 1e-6

WARM_BEFORE_X, WARM_AFTER_X = 8, 16
RING = 4
CW = 4 * 512
FFN_CHUNKS = 2 * UNITS + KF // 2
MIX_UNITS = 11
MIX_CHUNKS = 2 * MIX_UNITS + 2 * KD // 2
LAYER_CHUNKS = 2 * FFN_CHUNKS + MIX_CHUNKS
BASE = {"f1": 0, "m": FFN_CHUNKS, "f2": FFN_CHUNKS + MIX_CHUNKS}

Z0, XS0, DT0 = 0, 1024, 2560
Q0, K0, V0, G0 = 2576, 3088, 3600, 4624
MIX_COLS = [Q0, K0, XS0, XS0 + 512, XS0 + 1024, V0, V0 + 512, Z0, Z0 + 512, G0, G0 + 512]

C_ID, C_LE, C_GT, C_DM, C_QD, C_KD, C_IF, C_SUM = 0, 128, 256, 384, 896, 1408, 1412, 1476
N_CONST = C_SUM + HEADS
CUR_PRE = {"f1": 0, "m": 8, "f2": 16}
CUR_SSM, CUR_RET, CUR_CW, CUR_CB, CUR_DTB, CUR_NA, CUR_DS, N_CUR = 24, 32, 40, 88, 100, 116, 132, 148

N_PARAM = 16 * (3 + 1 + L)
MAGIC = 1.5 * 2.0 ** 23
ONE = 2 ** 100
INV_2PI = 15915494309189533576888376337251436203445964574046 * ONE // 10 ** 50
TWO_PI = 6.283185307179586


def parts(c, bits):
    out = []
    for b in bits:
        unit = ONE >> b
        n = (c + unit // 2) // unit
        out.append(n / 2 ** b)
        c -= n * unit
    return out


TURN_HIGH = parts(INV_2PI * 2 ** 15 % ONE, [7, 14, 21, 28])
TURN_LOW = parts(INV_2PI, [11, 20, 29])


EARLY = ["f1 normT00", "f1 normT0", "f1 uhi00", "f1 uhi01", "f1 ulo00", "f1 ulo01", "f1 presq0",
         "f1 pre0 mean", "f1 pre0"]


class Steps:

    def __init__(self, sem, known):
        self.sem, self.known, self.names, self.ahead = sem, known, [], 0

    def ahead_of_loop(self, name, last=False):
        if self.known is None:
            return 1
        to = len(self.known) if last else self.known[name]
        add, self.ahead = to - self.ahead, to
        return add

    def tick(self, name):
        assert name not in self.names, name
        self.names.append(name)
        return 1

    def at(self, name, l):
        if self.known is None:
            return l + 1
        if name in EARLY:
            l = l - 1
        return l * len(self.known) + (len(self.known) + self.known[name])

    def last(self, names):
        return names[0] if self.known is None else max(names, key=self.known.get)

    def result(self):
        return {n: i + 1 for i, n in enumerate(self.names)}


def by(i, step):
    return 0 if i is None else i * step


def cell_place(n):
    return (n % 2, n // 2) if n < TM_CELLS else (n // 2, n % 2)


WORK = [("rr", "act", "rr"), ("dt", "act", "dtf"), ("qT0", "act", "qT0"), ("kT0", "act", "kT0"),
        ("dtT", "dve", "dt in"), ("qT1", "act", "qT1"), ("kT1", "act", "kT1")]
WORK += [(f"xT{i}", "act", f"xT{i}") for i in range(2)]
WORK += [("sc0", "dve", "P0"), ("xT2", "act", "xT2"), ("sc1", "dve", "P1"), ("xT3", "act", "xT3")]
WORK += [("cb", "dve", "cb"), ("bT", "act", "bT"), ("dsum", "act", "ed"), ("df00", "act", "E00"),
         ("df01", "act", "E01"), ("df02", "act", "E02"),
         ("df03", "act", "E03"), ("yi00", "dve", "y00"), ("df10", "act", "E10"), ("yi01", "dve", "y01"),
         ("ss0", "act", "ss0"), ("ss1", "act", "ss1"), ("df11", "act", "E11"),
         ("df12", "act", "E12"), ("yi10", "dve", "y10"), ("yx0", "dve", "yx0"), ("df13", "act", "E13"),
         ("rs0", "act", "rs0"), ("rs1", "act", "rs1"), ("r00", "dve", "rn00"), ("r01", "dve", "rn01"),
         ("yi11", "dve", "y11"), ("yx1", "dve", "yx1"), ("r10", "dve", "rn10"), ("r11", "dve", "rn11")]
WORK += [(f"yT{j}", "dve", f"yT{j}") for j in range(4)] + [(f"rT{j}", "dve", f"rT{j}") for j in range(4)]
ORDER = [w[0] for w in WORK]
AFTER = {"rr": 3, "dt": 3, "qT0": 3, "kT0": 3, "dtT": 3, "qT1": 4, "kT1": 5, "xT0": 6, "xT1": 6,
         "sc0": 7, "xT2": 7, "sc1": 8, "xT3": 8, "cb": 11, "bT": 11, "dsum": 11, "df00": 12, "df01": 12, "df02": 13, "df03": 13,
         "yi00": 13, "df10": 14, "yi01": 14, "ss0": 14, "ss1": 14, "df11": 14, "rs0": 15, "rs1": 15,
         "df12": 15, "yi10": 15, "yx0": 15, "df13": 15, "r00": 16, "r01": 16, "yi11": 16, "yx1": 16,
         "r10": 17, "r11": 17, "yT0": 19, "yT1": 19, "yT2": 20, "yT3": 20}


def work_bank(name):
    i = ORDER.index(name)
    late = ORDER.index("yT0")
    return 4 + i % 4 if i < late else 4 + i % 2


def work_before(name):
    i = ORDER.index(name)
    for j in range(i - 1, -1, -1):
        if work_bank(ORDER[j]) == work_bank(name):
            return WORK[j]
    return None


MIX_CELL = ([("q", 0), ("k", 0), ("q", 1), ("k", 1)] + [("x", i) for i in range(4)] + [("b", 0), ("b", 1)]
            + [(a, i) for a in "vzg" for i in range(4)])
MIX_FREE = ([("dve", f"rot {a}{t}") for a, t in MIX_CELL[:4]] + [("dve", f"xr {m}") for m in range(4, 10)]
            + [("act", f"v{i}") for i in range(4)] + [("act", f"{a}{i}") for a in "zg" for i in range(4)])


def trunk(nc, a, known):
    with ExitStack() as ctx:
        def sb(name, shape, dt=F32, stack=ctx):
            return stack.enter_context(nc.sbuf_tensor(name, shape, dt))

        def sem(name):
            return ctx.enter_context(nc.semaphore(name))

        ps = ctx.enter_context(nc.psum_tensor("ps", [P, 8, 512], F32))

        raw = sb("raw", [P, RING, CW])
        w_hi = sb("w_hi", [P, RING, CW], F32R)
        w_lo = sb("w_lo", [P, RING, CW], F32R)
        x = sb("x", [P, T, D])
        u_hi = sb("u_hi", [P, KD, T * P], F32R)
        u_lo = sb("u_lo", [P, KD, T * P], F32R)
        tmp = sb("tmp", [P, 4, 512])
        tmp2 = tmp[:, :, :].rearrange("p (t a) n -> p t (a n)", t=T)
        post_w = sb("post_w", [P, D])
        const = sb("const", [P, N_CONST])
        cur = sb("cur", [P, N_CUR])
        cos = sb("cos", [P, T, 64])
        sin = sb("sin", [P, T, 64])
        rows = sb("rows", [104, P])
        rows_w = sb("rows_w", [96, P])
        bc = sb("bc", [P, 3, L, HEADS])
        dtw_raw = sb("dtw_raw", [P, L * KD * HEADS])
        dtw = sb("dtw", [P, KD, 2 * HEADS], F32R)
        na = sb("na", [P, HEADS])
        ssq = sb("ssq", [P, 8])
        ms = sb("ms", [P, 8])
        rstd = sb("rstd", [P, 8])
        neg_half = sb("neg_half", [P, 8])
        pos_i = sb("pos_i", [P, T], I32)
        pos_f = sb("pos_f", [P, T])

        with ExitStack() as ffn_only:
            h_hi = sb("h_hi", [P, KF, T * P], F32R, ffn_only)
            h_lo = sb("h_lo", [P, KF, T * P], F32R, ffn_only)
            gate = sb("gate", [P, 2, UW], F32, ffn_only)
            hh = sb("hh", [P, 2, UW], F32, ffn_only)
            turn = sb("turn", [P, 7, T * 64], F32, ffn_only)
            tmpp = sb("tmpp", [P, 10, T * 64], F32, ffn_only)
            rrow_f = sb("rrow_f", [P, T * P], F32, ffn_only)
            first_rows = sb("first_rows", [L * KD, P], F32, ffn_only)
            zeros = sb("zeros", [P, 512], mybir.dt.bfloat16, ffn_only)
            unused = sb("unused", [P, 1], F32, ffn_only)
        with ExitStack() as under_y:
            qT = sb("qT", [P, RH, T * P], F32, under_y)
            kT = sb("kT", [P, RH, T * P], F32, under_y)
            bcf = sb("bcf", [P, 4, T * P], F32, under_y)
            btok = sb("btok", [P, GROUPS, P], F32, under_y)
            mcb = sb("mcb", [P, T, GROUPS, P], F32, under_y)
            rrow = sb("rrow", [P, T * P], F32, under_y)
        y_hi = sb("y_hi", [P, KD, T * P], F32R)
        y_lo = sb("y_lo", [P, KD, T * P], F32R)
        ys = sb("ys", [P, T, D])
        vr = sb("vr", [P, T, D])
        kdt = sb("kdt", [P, RH, P])
        qdT = qT[:, :, P:2 * P]
        xdt = sb("xdt", [P, T, D])
        xde = post_w
        state = sb("state", [P, GROUPS, 512])
        with ExitStack() as under_rstate:
            uda1 = sb("uda1", [P, 2, 4, P], F32R, under_rstate)
        rstate = sb("rstate", [P, RH, RV])
        uda0 = sb("uda0", [P, 2, 4, P], F32R)
        gt_r = sb("gt_r", [P, P], F32R)
        em = sb("em", [P, 2, 4, P])
        dtf = em[0:2 * HEADS, 0, 0:T, :]
        pr = sb("pr", [P, T, RH, P])
        dts = sb("dts", [P, 10, T * HEADS])
        da_hi = sb("da_hi", [P, T * HEADS], F32R)
        da_lo = sb("da_lo", [P, T * HEADS], F32R)
        dtr, nab, ex, z1, z2, zq, dt, da, ed, dmx = (dts[:, i, :] for i in range(10))
        bn = sb("bn", [P, T, RH, 6])
        mv = sb("mv", [P, T, RH, 2])
        gv = sb("gv", [P, T, RH])
        grs = sb("grs", [P, T, RH])

        bcf_flat = bc[:, :, :, :].rearrange("p i l h -> p (i l h)")
        ident = const[:, C_ID:C_ID + P]
        le = const[:, C_LE:C_LE + P]
        gt = const[:, C_GT:C_GT + P]

        x_in = [sem(f"x_in{t}") for t in range(T)]
        x_in_half = sem("x_in_half")
        ident_in = sem("ident_in")
        norm_rows_in = sem("norm_rows_in")
        const_in = sem("const_in")
        param_in = sem("param_in")
        raw_landed = [sem(f"raw_landed{i}") for i in range(RING)]
        half_hi = sem("half_hi")
        hi_done = sem("hi_done")
        lo_done = sem("lo_done")
        weights_used = sem("weights_used")
        post_w_in = sem("post_w_in")
        post_w_free = sem("post_w_free")
        cell_filled = sem("cell_filled")
        gate_scaled = sem("gate_scaled")
        gate_ready = sem("gate_ready")
        h_ready = sem("h_ready")
        hT_filled = sem("hT_filled")
        hT_hi = sem("hT_hi")
        hT_lo = sem("hT_lo")
        setup_pe = sem("setup_pe")
        setup_act = sem("setup_act")
        setup_pool = sem("setup_pool")
        stored = sem("stored")
        sp_waited = sem("sp_waited")
        pool_waited = sem("pool_waited")
        dve_waited = sem("dve_waited")
        S = {}
        for e in ("pe", "act", "dve", "pool"):
            S[e] = Steps(sem(f"{e}_steps"), known and known[e])
        PE, AC, DV, PO = S["pe"], S["act"], S["dve"], S["pool"]

        block = ctx.enter_context(nc.Block())

        def uda(i, part):
            return (uda0, uda1)[i % 2][:, part, :, :]

        def ffn_value(f, l, n, ahead=0):
            return l * (2 * CELLS) + (f == "f2") * CELLS + n + 1 + ahead

        def turned_value(f, l, n):
            return (2 * l + (f == "f2")) * TM_CELLS + n + 1

        def scaled_value(f, l, n):
            return (2 * l + (f == "f2")) * (CELLS - TM_CELLS) + n - TM_CELLS + 1

        def chunk_value(s, l, c, ahead=0):
            return l * LAYER_CHUNKS + BASE[s] + c + 1 + ahead

        def slot_of(s, c):
            return (BASE[s] + c) % RING

        def wait_steps(eng, l, needs):
            for st in S.values():
                names = [n for s_, n in needs if s_ is st]
                if names:
                    eng.wait_ge(st.sem, st.at(st.last(names), l))

        @block.sync
        def _(sp):
            sp.dma_start(x[:, 0, 0:D // 2], a["x"][0, 0:P, 0:D // 2]).then_inc(x_in[0], 16)

            def wait_apart(sem_, value):
                sp.wait_ge(sem_, value)
                sp.sem_inc(sp_waited, 1)

            def chunk(s, l, c, halves, i=None):
                slot = slot_of(s, c)
                wait_apart(lo_done, chunk_value(s, l, c) + by(i, 4))
                for dst, src in halves:
                    sp.dma_start(dst, src).then_inc(raw_landed[slot], 16)

            def post_weights(s, l, n):
                wait_apart(post_w_free, l * 3 + n + 1)
                row = a[{"f1": "ffn1_post_norm", "m": "mix_post_norm", "f2": "ffn2_post_norm"}[s]][bass.ds(l, 1), :]
                sp.dma_start(post_w[:, :], row.broadcast_to([P, D])
                             ).then_inc(post_w_in, 16)

            def gate_up(s, l, w, c, i=None):
                u, kh = c // 2, c % 2
                dst = raw[:, slot_of(s, c), :].rearrange("p (k g n) -> p k g n", k=4, g=2)
                halves = []
                for g in range(2):
                    src = w[bass.ds(l, 1), kh * 512:(kh + 1) * 512, bass.ds(g * FF + u * UW + by(i, 2 * UW), UW)]
                    halves.append((dst[:, :, g, :], src.rearrange("a (k p) n -> p (a k) n", p=P)))
                chunk(s, l, c, halves, i)

            def down(s, l, w, first, j, i=None):
                c = first + j
                dst = raw[:, slot_of(s, c), :].rearrange("p (k n) -> p k n", k=2)
                halves = []
                for k in range(2):
                    src = w[bass.ds(l, 1), bass.ds((2 * j + k) * P + by(i, 8 * P), P), :]
                    halves.append((dst[:, k, :], src.rearrange("a p n -> (a p) n")))
                chunk(s, l, c, halves, i)

            def ffn(s, l, n):
                w1, w2 = a[f"ffn{s[1]}_w_in"], a[f"ffn{s[1]}_w_out"]
                with sp.Fori(0, 5) as i:
                    for c in range(4):
                        gate_up(s, l, w1, c, i)
                for c in range(20, 22):
                    gate_up(s, l, w1, c)
                post_weights(s, l, n)
                with sp.Fori(0, 2) as i:
                    for j in range(4):
                        down(s, l, w2, CELLS, j, i)
                for j in range(8, 11):
                    down(s, l, w2, CELLS, j)

            def mixer(l):
                for c in range(2 * MIX_UNITS):
                    u, kh = c // 2, c % 2
                    dst = raw[:, slot_of("m", c), :].rearrange("p (k n) -> p k n", k=4)
                    halves = []
                    for h in range(2):
                        r = kh * 512 + h * 256
                        src = a["mix_w_in"][bass.ds(l, 1), r:r + 256, MIX_COLS[u]:MIX_COLS[u] + 512]
                        halves.append((dst[:, 2 * h:2 * h + 2, :], src.rearrange("a (k p) n -> p (a k) n", p=P)))
                    chunk("m", l, c, halves)
                wait_apart(PE.sem, PE.at("ss1", l))
                post_weights("m", l, 1)
                for j in range(8):
                    down("m", l, a["mix_w_out"], 2 * MIX_UNITS, j)

            with sp.Fori(0, L) as l:
                ffn("f1", l, 0)
                mixer(l)
                ffn("f2", l, 2)
            for t in range(T):
                for h in range(2):
                    cols = slice(h * 512, (h + 1) * 512)
                    sp.wait_ge(DV.sem, DV.at(f"f2 res{t}" + ("" if h else " half"), L - 1))
                    sp.dma_start(a["out"][0, t * P:(t + 1) * P, cols], x[:, t, cols]).then_inc(stored, 16)
            sp.wait_ge(stored, 64)

        @block.gpsimd
        def _(pool):
            pool.memset(neg_half[:, :], -0.5).then_inc(setup_pool, 1)
            pool.memset(zeros[:, :], 0.0).then_inc(setup_pool, 1)
            names = ["ffn1_pre_norm", "mix_pre_norm", "ffn2_pre_norm", "ssm_norm", "ret_norm"]
            for i, n in enumerate(names):
                pool.dma_start(rows[16 * i:16 * i + 16, :],
                               a[n].rearrange("l (k p) -> (l k) p", p=P)).then_inc(norm_rows_in, 16)
            pool.dma_start(rows[80:104, :], a["conv_b"].rearrange("l (k p) -> (l k) p", p=P)).then_inc(norm_rows_in, 16)
            pool.dma_start(rows_w[:, :], a["conv_w"].rearrange("l j (k p) -> (l j k) p", p=P)).then_inc(norm_rows_in, 16)
            pool.dma_start(const[:, P:], a["const"][:, P:]).then_inc(const_in, 16)
            for i, n in enumerate(["dt_bias", "a_log", "d_skip"]):
                src = a[n].rearrange("l h -> (l h)").unsqueeze(0).broadcast_to([P, L * HEADS])
                pool.dma_start(bc[:, i, :, :].rearrange("p l h -> p (l h)"), src).then_inc(param_in, 16)
            with nc.allow_non_contiguous_dma(reason="positions as a column, once"):
                pool.dma_start(pos_i[:, :], a["positions"].rearrange("a (t p) -> p (a t)", p=P)).then_inc(param_in, 16)
            for l in range(L):
                pool.dma_start(dtw_raw[:, l * KD * HEADS:(l + 1) * KD * HEADS].rearrange("p (k h) -> p k h", k=KD),
                               a["mix_w_in"][l, :, DT0:DT0 + HEADS].rearrange("(k p) h -> p k h", p=P)).then_inc(param_in, 16)
            pool.wait_ge(setup_pool, 1)

            def wait_apart(sem_, value):
                pool.wait_ge(sem_, value)
                pool.sem_inc(pool_waited, 1)

            def inv_root(l, name, j, src, waits, scale, eps, n=1, srct=None, mst=None, out=None, ahead=False):
                for st, step in waits:
                    wait_apart(st.sem, st.at(step, l))
                srct = ssq[:, j:j + n] if srct is None else srct
                mst = ms[:, j:j + n] if mst is None else mst
                out = rstd[:, j:j + n] if out is None else out
                pool.tensor_scalar(mst, srct, scale, eps, ALU.mult, ALU.add).then_inc(
                    PO.sem, PO.ahead_of_loop(name + " mean") if ahead else PO.tick(name + " mean"))
                wait_apart(PO.sem, PO.at(name + " mean", l))
                pool.tensor_tensor(out, mst, neg_half[:, 0:n], ALU.pow).then_inc(
                    PO.sem, PO.ahead_of_loop(name, last=True) if ahead else PO.tick(name))

            def post(l, s, t):
                if s == "m":
                    inv_root(l, f"m post{t}", t, None, [(AC, f"m postsq{t}")], 1.0 / D, EPS)
                    return
                mine(l, f"{s} pre{t}")
                op(l, f"{s} eps{t}", pool.tensor_scalar(ms[:, 6 + t:7 + t], ms[:, 2 + t:3 + t], 4 * EPS, None, ALU.mult))
                mine(l, f"{s} eps{t}")
                inv_root(l, f"{s} post{t}", t, None, [(AC, f"{s} postsq{t}")], 4.0 / D, ms[:, 6 + t:7 + t])

            def pre(l, s, t):
                inv_root(l, f"{s} pre{t}", 2 + t, None, [(AC, f"{s} presq{t}")], 1.0 / D, EPS)

            def op(l, name, ins):
                ins.then_inc(PO.sem, PO.tick(name))
                return name

            def mine(l, name):
                wait_apart(PO.sem, PO.at(name, l))

            def phases(l):
                mine(l, "f1 pre1")
                pool.wait_ge(param_in, N_PARAM)
                pool.wait_ge(const_in, 16)
                keep = tmpp
                op(l, "ph pos", pool.tensor_copy(pos_f[:, :], pos_i[:, :]))
                mine(l, "ph pos")
                for t in range(T):
                    n = op(l, f"ph ang{t}", pool.tensor_scalar(
                        keep[:, 0, t * 64:(t + 1) * 64], const[:, C_IF:C_IF + 64], pos_f[:, t:t + 1], None, ALU.mult))
                mine(l, n)
                op(l, "ph h0", pool.tensor_scalar(keep[:, 1, :], keep[:, 0, :], 2.0 ** -15, MAGIC, ALU.mult, ALU.add))
                mine(l, "ph h0")
                op(l, "ph h1", pool.tensor_scalar(keep[:, 1, :], keep[:, 1, :], MAGIC, None, ALU.subtract))
                mine(l, "ph h1")
                op(l, "ph h2", pool.tensor_scalar(keep[:, 2, :], keep[:, 1, :], 2.0 ** 15, None, ALU.mult))
                mine(l, "ph h2")
                op(l, "ph l0", pool.tensor_tensor(keep[:, 0, :], keep[:, 0, :], keep[:, 2, :], ALU.subtract))
                mine(l, "ph l0")
                op(l, "ph l1", pool.tensor_scalar(keep[:, 2, :], keep[:, 0, :], MAGIC, MAGIC, ALU.add, ALU.subtract))
                mine(l, "ph l1")
                op(l, "ph f0", pool.tensor_tensor(keep[:, 0, :], keep[:, 0, :], keep[:, 2, :], ALU.subtract))
                for i, c in enumerate(TURN_HIGH):
                    n = op(l, f"ph p{i}", pool.tensor_scalar(turn[:, i, :], keep[:, 1, :], c, None, ALU.mult))
                for i, c in enumerate(TURN_LOW):
                    n = op(l, f"ph p{4 + i}", pool.tensor_scalar(turn[:, 4 + i, :], keep[:, 2, :], c, None, ALU.mult))
                mine(l, n)
                op(l, "ph r", pool.tensor_scalar(keep[:, 3:10, :], turn[:, :, :], MAGIC, MAGIC, ALU.add, ALU.subtract))
                mine(l, "ph r")
                op(l, "ph fr", pool.tensor_tensor(turn[:, :, :], turn[:, :, :], keep[:, 3:10, :], ALU.subtract))
                op(l, "ph af", pool.tensor_scalar(keep[:, 0, :], keep[:, 0, :], INV_2PI / ONE, None, ALU.mult))
                mine(l, "ph af")
                for i in range(7):
                    n = op(l, f"ph s{i}", pool.tensor_tensor(keep[:, 0, :], keep[:, 0, :], turn[:, i, :], ALU.add))
                    mine(l, n)
                op(l, "ph c0", pool.tensor_scalar(keep[:, 1, :], keep[:, 0, :], 0.25, None, ALU.add))
                mine(l, "ph c0")
                op(l, "ph r2", pool.tensor_scalar(keep[:, 2:4, :], keep[:, 0:2, :], MAGIC, MAGIC, ALU.add, ALU.subtract))
                mine(l, "ph r2")
                op(l, "phases", pool.tensor_tensor(keep[:, 0:2, :], keep[:, 0:2, :], keep[:, 2:4, :], ALU.subtract))

            def rotate(l, q, t, par_):
                wait_apart(DV.sem, DV.at(f"rot {q}{t}", l))
                A = tmp[:, 0, :].rearrange("p (h a d) -> p h a d", h=RH, a=2)
                B = tmp[:, 1, :].rearrange("p (h a d) -> p h a d", h=RH, a=2)
                O = tmp[:, 2 + par_, :].rearrange("p (h a d) -> p h a d", h=RH, a=2)
                if t == 1:
                    wait_apart(PE.sem, PE.at(f"{q}T0", l))
                    if q == "k":
                        mine(l, "kdt")
                op(l, f"rota {q}{t}", pool.tensor_tensor(O[:, :, 0, :], A[:, :, 0, :], B[:, :, 1, :], ALU.subtract))
                op(l, f"rot {q}{t}", pool.tensor_tensor(O[:, :, 1, :], A[:, :, 1, :], B[:, :, 0, :], ALU.add))

            def bcast_heads(tile, t, n0=0, n=HEADS):
                return tile[:, t * HEADS + n0:t * HEADS + n0 + n].unsqueeze(2).broadcast_to([P, n, HP])

            def x_heads(tile):
                return tile.rearrange("p (h d) -> p h d", d=HP)

            def decays(l, c, q, i):
                if i >= 2:
                    wait_apart(PE.sem, PE.at(f"df{(i - 2) // 4}{(i - 2) % 4}", l))
                wait_apart(DV.sem, DV.at("da lo", l))
                for part, tile in enumerate((da_hi, da_lo)):
                    d = tile[:, c * HEADS + 4 * q:c * HEADS + 4 * q + 4].bitcast(F32).unsqueeze(2).broadcast_to([P, 4, P])
                    op(l, f"uda{c}{q}" + " lo" * part, pool.tensor_tensor(
                        uda(i, part), le.unsqueeze(1).broadcast_to([P, 4, P]), d, ALU.mult))

            inv_root(0, "f1 pre0", 2, None, [(AC, "f1 presq0")], 1.0 / D, EPS, ahead=True)
            with pool.Fori(0, L) as l:
                pre(l, "f1", 1)
                phases(l)
                for t in range(T):
                    post(l, "f1", t)
                for t in range(T):
                    pre(l, "m", t)
                rotate(l, "q", 0, 0)
                rotate(l, "k", 0, 1)
                mine(l, "rot k0")
                op(l, "kdt", pool.tensor_tensor(
                    kdt[:, :, :], tmp[:, 3, :].rearrange("p (h d) -> p h d", h=RH),
                    const[:, C_KD:C_KD + RH].unsqueeze(2).broadcast_to([P, RH, P]), ALU.mult))
                rotate(l, "q", 1, 0)
                rotate(l, "k", 1, 1)
                decays(l, 0, 0, 0)
                decays(l, 0, 1, 1)
                wait_apart(AC.sem, AC.at("xT3", l))
                op(l, "xdt0", pool.tensor_tensor(x_heads(xdt[:, 0, :]), x_heads(ys[:, 0, :]), bcast_heads(dt, 0), ALU.mult))
                decays(l, 0, 2, 2)
                decays(l, 0, 3, 3)
                wait_apart(PE.sem, PE.at("sc1", l))
                op(l, "qdT", pool.tensor_tensor(
                    qdT, qdT, const[:, C_QD:C_QD + RH * P].rearrange("p (h d) -> p h d", h=RH), ALU.mult))
                wait_apart(AC.sem, AC.at("ed", l))
                mine(l, "xdt0")
                op(l, "xde", pool.tensor_tensor(x_heads(xde[:, :]), x_heads(xdt[:, 0, :]), bcast_heads(ed, 0), ALU.mult))
                skip = cur[:, CUR_DS:CUR_DS + HEADS].unsqueeze(2).broadcast_to([P, HEADS, HP])
                op(l, "skip0", pool.tensor_tensor(x_heads(ys[:, 0, :]), x_heads(ys[:, 0, :]), skip, ALU.mult))
                decays(l, 1, 0, 4)
                decays(l, 1, 1, 5)
                op(l, "xdt1", pool.tensor_tensor(x_heads(xdt[:, 1, :]), x_heads(ys[:, 1, :]), bcast_heads(dt, 1), ALU.mult))
                mine(l, "xdt1")
                op(l, "skip1", pool.tensor_tensor(x_heads(ys[:, 1, :]), x_heads(ys[:, 1, :]), skip, ALU.mult))
                decays(l, 1, 2, 6)
                decays(l, 1, 3, 7)
                for t in range(T):
                    inv_root(l, f"gn{t}", 0, None, [(DV, f"mv{t}")], 1.0, 1e-5, RH,
                             mv[:, t, :, 1], gv[:, t, :], grs[:, t, :])
                for t in range(T):
                    inv_root(l, f"ssm rs{t}", 4 + t, None, [(AC, f"ysq{t}")], 1.0 / D, EPS)
                for t in range(T):
                    post(l, "m", t)
                for t in range(T):
                    pre(l, "f2", t)
                for t in range(T):
                    post(l, "f2", t)
                pre(l + 1, "f1", 0)

        @block.scalar
        def _(act):
            act.wait_ge(setup_pool, 1)
            act.activation(unused[:, :], neg_half[:, 0:1], ACT.Silu).then_inc(setup_act, 1)
            act.dma_start(const[:, 0:P], a["const"][:, 0:P]).then_inc(ident_in, 16)
            act.dma_start(first_rows[:, :], a["ffn1_pre_norm"].rearrange("l (k p) -> (l k) p", p=P)).then_inc(ident_in, 16)
            act.dma_start(x[:, 0, D // 2:], a["x"][0, 0:P, D // 2:]).then_inc(x_in_half, 16)

            def split(s, l, c, i=None):
                slot = slot_of(s, c)
                act.wait_ge(raw_landed[slot], l * (32 * LAYER_CHUNKS // RING) + by(i, 32)
                            + 32 * ((BASE[s] + c) // RING + 1))
                act.wait_ge(weights_used, chunk_value(s, l, c) + by(i, 4))
                act.activation(w_hi[:, slot, :], raw[:, slot, :], ACT.Copy).then_inc(hi_done, 1)

            def wait(st, name, l):
                act.wait_ge(st.sem, st.at(name, l))

            def postsq(l, s, t):
                b = 2 + 4 * t
                wait(PE, f"{s} acc{t}", l)
                act.activation(tmp2[:, t, :], ps[:, b:b + 2, :].rearrange("p a n -> p (a n)"), ACT.Square,
                               accum_out=ssq[:, t:t + 1]).then_inc(AC.sem, AC.tick(f"{s} postsq{t}"))

            def presq(l, s, t, ahead=False):
                act.wait_ge(x_in[t], 16)
                if ahead:
                    act.wait_ge(x_in_half, 16)
                else:
                    before, lb = {"f1": ("f2", l - 1), "m": ("f1", l), "f2": ("m", l)}[s]
                    wait(DV, f"{before} res{t}", lb)
                act.activation(tmp2[:, t, :], x[:, t, :], ACT.Square, accum_out=ssq[:, 2 + t:3 + t]).then_inc(
                    AC.sem, AC.ahead_of_loop("f1 presq0", last=True) if ahead else AC.tick(f"{s} presq{t}"))

            def norm_hi(l, s, t, ahead=False, halves=(0, 1)):
                if (s, t) == ("f1", 0) and not ahead:
                    wait(DV, "cur next", l - 1)
                for b in halves:
                    wait(PE, f"{s} normT{t}{b}" if b == 0 else f"{s} normT{t}", l)
                    for k in range(4):
                        kk = 4 * b + k
                        col = CUR_PRE[s] + kk
                        ins = act.activation(u_hi[:, kk, t * P:(t + 1) * P], ps[:, 4 + 2 * t + b, k * P:(k + 1) * P],
                                             ACT.Copy, scale=cur[:, col:col + 1])
                    name = f"{s} uhi{t}{b}"
                    ins.then_inc(AC.sem, AC.ahead_of_loop(name) if ahead else AC.tick(name))

            def silu(s, l, m, i=None):
                if m < TM_CELLS:
                    act.wait_ge(cell_filled, ffn_value(s, l, m))
                    act.wait_ge(h_ready, ffn_value(s, l, m - 2, 4))
                    t = cell_place(m)[1]
                    if m in (0, 2):
                        wait(PO, f"{s} pre{t}", l)
                    act.activation(gate[:, m % 2, :], ps[:, m % 4, 0:UW], ACT.Silu,
                                   scale=rstd[:, 2 + t:3 + t]).then_inc(gate_ready, 1)
                else:
                    act.wait_ge(gate_scaled, scaled_value(s, l, m) + by(i, 4))
                    act.activation(gate[:, m % 2, :], gate[:, m % 2, :], ACT.Silu).then_inc(gate_ready, 1)

            def enter(l, s, before):
                postsq(l, before, 0)
                split(s, l, 0)
                norm_hi(l, s, 0)
                split(s, l, 1)
                split(s, l, 2)
                postsq(l, before, 1)
                presq(l, s, 0)
                enter_rest(l, s)

            def enter_rest(l, s):
                split(s, l, 3)
                if s != "m":
                    silu(s, l, 0)
                norm_hi(l, s, 1)
                presq(l, s, 1)

            def end_layer(l):
                postsq(l, "f2", 0)
                with act.If(l < L - 1):
                    split("f1", l + 1, 0)
                norm_hi(l + 1, "f1", 0)
                with act.If(l < L - 1):
                    split("f1", l + 1, 1)
                    split("f1", l + 1, 2)
                postsq(l, "f2", 1)
                presq(l + 1, "f1", 0)

            def ffn(s, l):
                def h_hi_part(m, i=None):
                    if m < TM_CELLS:
                        u, t = cell_place(m)
                        act.wait_ge(hT_filled, turned_value(s, l, m))
                        act.activation(h_hi[:, 2 * u:2 * u + 2, t * P:(t + 1) * P],
                                       ps[:, 4 + m % 2, 0:UW].rearrange("p (k n) -> p k n", k=2),
                                       ACT.Copy).then_inc(hT_hi, 1)
                    else:
                        act.wait_ge(h_ready, ffn_value(s, l, m, 4) + by(i, 4))
                        act.activation(h_hi[:, bass.ds(m + by(i, 4), 1), :], hh[:, m % 2, :].unsqueeze(1),
                                       ACT.Copy).then_inc(hT_hi, 1)

                def slot(n, i=None):
                    if n - 1 >= TM_CELLS and n + 2 < FFN_CHUNKS:
                        split(s, l, n + 2, i)
                    if 2 <= n <= CELLS + 1 and n - 2 >= TM_CELLS:
                        h_hi_part(n - 2, i)
                    if 2 <= n <= CELLS:
                        silu(s, l, n - 1, i)
                    if 2 <= n and n - 2 < TM_CELLS:
                        h_hi_part(n - 2, i)
                    if n == 3:
                        wait(PE, f"{s} rr", l)
                        act.copy(rrow_f[:, :], ps[:, 6, 0:T * P]).then_inc(AC.sem, AC.tick(f"{s} rr"))
                    if 4 <= n + 2 and n - 1 < TM_CELLS:
                        split(s, l, n + 2, i)

                for n in range(6):
                    slot(n)
                with act.Fori(0, 3) as i:
                    for n in range(6, 10):
                        slot(n, i)
                for n in range(18, FFN_CHUNKS - 2):
                    slot(n)

            def mixer(l):
                def cell(m, s="m"):
                    act.wait_ge(PE.sem, PE.at(f"cell{m}", l))

                def done(name, ins):
                    ins.then_inc(AC.sem, AC.tick(name))

                def item(name):
                    wait(PE, name, l)
                    return ps[:, work_bank(name), :]

                def qk(a_, t):
                    src = item(f"{a_}T{t}").rearrange("p (h n) -> p h n", h=RH)
                    dst = (qT if a_ == "q" else kT)[:, :, t * P:(t + 1) * P]
                    done(f"{a_}T{t}", act.copy(dst, src))

                def conv_silu(m):
                    wait(DV, f"conv {m}", l)
                    cs = tmp[:, m % 2, :]
                    dst = cs if m < 8 else bcf[:, 2 * (m - 8):2 * (m - 8) + 2, :].rearrange("p f n -> p (f n)")
                    done(f"silu {m}", act.activation(dst, cs, ACT.Silu))

                def x_tok(i):
                    src = item(f"xT{i}").rearrange("p (t n) -> p t n", t=T)
                    done(f"xT{i}", act.copy(ys[:, :, i * 256:(i + 1) * 256], src))

                def decay_exp(c, q):
                    i = 4 * c + q
                    need = [(PE, f"df{c}{q}")]
                    if i >= 2:
                        j = i - 2
                        need.append((PE, f"yi{j // 4}{(j % 4) // 2}" + ("h" if j % 2 == 0 else "")))
                    wait_steps(act, l, need)
                    src = ps[:, work_bank(f"df{c}{q}"), :].rearrange("p (h n) -> p h n", h=4)
                    done(f"E{c}{q}", act.activation(em[:, i % 2, :, :], src, ACT.Exp))

                def gate_silu(a_, i):
                    m = {"z": 14, "g": 18}[a_] + i
                    cell(m)
                    if a_ == "g":
                        wait(DV, f"z{i}", l)
                    else:
                        wait(AC, "silu 9", l)
                    done(f"{a_}{i}", act.activation(tmp[:, i, :], ps[:, m % 4, :], ACT.Silu,
                                                    scale=rstd[:, 2 + i % 2:3 + i % 2]))

                def v_copy(i):
                    cell(10 + i)
                    half, t = i // 2, i % 2
                    done(f"v{i}", act.activation(vr[:, t, half * 512:(half + 1) * 512], ps[:, (10 + i) % 4, :],
                                                 ACT.Copy, scale=rstd[:, 2 + t:3 + t]))

                def y_square(t):
                    wait(DV, f"z{2 + t}", l)
                    done(f"ysq{t}", act.activation(xdt[:, t, :], ys[:, t, :], ACT.Square, accum_out=ssq[:, 4 + t:5 + t]))

                def yT(a_, j):
                    src = item(f"{a_}T{j}")
                    for kk in range(2):
                        k = 2 * j + kk
                        dst, col = (y_hi, CUR_SSM) if a_ == "y" else (u_hi, CUR_RET)
                        ins = act.activation(dst[:, k, :], src[:, kk * 256:(kk + 1) * 256], ACT.Copy,
                                             scale=cur[:, col + k:col + k + 1])
                    done(f"{a_}T{j}", ins)

                def sp_(n):
                    if 4 <= n + 2 < MIX_CHUNKS:
                        split("m", l, n + 2)

                for n in range(5):
                    sp_(n)
                    if n == 4:
                        done("rr", act.copy(rrow[:, :], item("rr")[:, 0:T * P]))
                        done("dtf", act.copy(dtf, item("dt")[0:2 * HEADS, 0:T * P].rearrange("p (t n) -> p t n", t=T)))
                        qk("q", 0)
                        qk("k", 0)
                        wait(DV, "nab", l)
                        done("na", act.activation(na[:, :], cur[:, CUR_NA:CUR_NA + HEADS], ACT.Exp))
                        done("ex", act.activation(ex, nab, ACT.Exp))
                sp_(5)
                qk("q", 1)
                conv_silu(4)
                sp_(6)
                qk("k", 1)
                conv_silu(5)
                x_tok(0)
                sp_(7)
                conv_silu(6)
                x_tok(1)
                sp_(8)
                conv_silu(7)
                x_tok(2)
                sp_(9)
                conv_silu(8)
                x_tok(3)
                sp_(10)
                conv_silu(9)
                sp_(11)
                v_copy(0)
                done("bT", act.copy(btok[:, :, :], item("bT")[:, 0:256].rearrange("p (g n) -> p g n", g=GROUPS)))
                wait(PE, "dsum", l)
                done("ed", act.activation(ed, ps[:, work_bank("dsum"), 0:T * HEADS], ACT.Exp))
                decay_exp(0, 0)
                sp_(12)
                v_copy(1)
                decay_exp(0, 1)
                sp_(13)
                v_copy(2)
                decay_exp(0, 2)
                decay_exp(0, 3)
                sp_(14)
                v_copy(3)
                decay_exp(1, 0)
                for g in range(GROUPS):
                    done(f"ss{g}", act.copy(state[:, g, :], item(f"ss{g}")))
                sp_(15)
                decay_exp(1, 1)
                decay_exp(1, 2)
                sp_(16)
                decay_exp(1, 3)
                for i in range(2):
                    done(f"rs{i}", act.copy(rstate[:, 2 * i:2 * i + 2, :].rearrange("p h n -> p (h n)"), item(f"rs{i}")))
                gate_silu("z", 0)
                sp_(17)
                gate_silu("z", 1)
                sp_(18)
                gate_silu("z", 2)
                gate_silu("z", 3)
                sp_(19)
                gate_silu("g", 0)
                y_square(0)
                y_square(1)
                sp_(20)
                gate_silu("g", 1)
                for j in range(2):
                    yT("y", j)
                sp_(21)
                gate_silu("g", 2)
                sp_(22)
                gate_silu("g", 3)
                for j in range(2, 4):
                    yT("y", j)
                for j in range(2):
                    yT("r", j)
                sp_(23)
                for j in range(2, 4):
                    yT("r", j)
                for n in range(24, MIX_CHUNKS - 2):
                    sp_(n)

            act.wait_ge(setup_pe, 1)
            act.copy(cur[:, 0:8], ps[:, 0, 0:8]).then_inc(setup_act, 1)
            act.wait_ge(setup_act, 2)
            norm_hi(0, "f1", 0, ahead=True, halves=[0])
            act.wait_ge(raw_landed[0], 32)
            for h in range(2):
                act.activation(w_hi[:, 0, h * CW // 2:(h + 1) * CW // 2], raw[:, 0, h * CW // 2:(h + 1) * CW // 2],
                               ACT.Copy).then_inc(hi_done if h else half_hi, 1)
            norm_hi(0, "f1", 0, ahead=True, halves=[1])
            act.dma_start(x[:, 1, :], a["x"][0, P:2 * P, :]).then_inc(x_in[1], 16)
            split("f1", 0, 1)
            split("f1", 0, 2)
            presq(0, "f1", 0, ahead=True)
            with act.Fori(0, L) as l:
                enter_rest(l, "f1")
                ffn("f1", l)
                wait(PO, "phases", l)
                act.activation(sin[:, :, :], tmpp[:, 0, :].rearrange("p (t n) -> p t n", t=T), ACT.Sin,
                               scale=TWO_PI).then_inc(AC.sem, AC.tick("sin"))
                act.activation(cos[:, :, :], tmpp[:, 1, :].rearrange("p (t n) -> p t n", t=T), ACT.Sin,
                               scale=TWO_PI).then_inc(AC.sem, AC.tick("cos"))
                enter(l, "m", "f1")
                mixer(l)
                enter(l, "f2", "m")
                ffn("f2", l)
                end_layer(l)

        @block.vector
        def _(dve):
            dve.sem_inc(lo_done, RING)
            dve.sem_inc(h_ready, 4)
            dve.sem_inc(hT_lo, 2)
            dve.sem_inc(post_w_free, 1)

            def split(s, l, c, i=None):
                slot = slot_of(s, c)
                dve.wait_ge(hi_done, chunk_value(s, l, c) + by(i, 4))
                dve.tensor_tensor(w_lo[:, slot, :], raw[:, slot, :], w_hi[:, slot, :].bitcast(F32),
                                  ALU.subtract).then_inc(lo_done, 1)

            def wait(st, name, l):
                dve.wait_ge(st.sem, st.at(name, l))

            def done(name, ins):
                ins.then_inc(DV.sem, DV.tick(name))

            def chain(name, l, ins):
                ins.then_inc(DV.sem, DV.tick(name))
                dve.wait_ge(DV.sem, DV.at(name, l))

            def residual(l, s, n, t):
                b = 2 + 4 * t
                wait(PO, f"{s} post{t}", l)
                dve.wait_ge(post_w_in, l * 48 + 16 * (n + 1))
                halves = [slice(h * 512, (h + 1) * 512) for h in range(2)]
                for h, cols in enumerate(halves):
                    done(f"{s} scaled{t}{h}", dve.scalar_tensor_tensor(
                        tmp2[:, t, cols], ps[:, b + h, :], rstd[:, t:t + 1], post_w[:, cols], ALU.mult, ALU.mult))
                for h, cols in enumerate(halves):
                    wait(DV, f"{s} scaled{t}{h}", l)
                    done(f"{s} res{t}" + ("" if h else " half"),
                         dve.tensor_tensor(x[:, t, cols], x[:, t, cols], tmp2[:, t, cols], ALU.add))
                if t == 1:
                    dve.sem_inc(post_w_free, 1)

            def norm_lo(l, s, t, ahead=False, halves=(0, 1)):
                for b in halves:
                    wait(AC, f"{s} uhi{t}{b}", l)
                    for k in range(4):
                        kk = 4 * b + k
                        col = CUR_PRE[s] + kk
                        ins = dve.scalar_tensor_tensor(
                            u_lo[:, kk, t * P:(t + 1) * P], ps[:, 4 + 2 * t + b, k * P:(k + 1) * P],
                            cur[:, col:col + 1], u_hi[:, kk, t * P:(t + 1) * P].bitcast(F32), ALU.mult, ALU.subtract)
                    if ahead:
                        ins.then_inc(DV.sem, DV.ahead_of_loop(f"{s} ulo{t}{b}", last=b == 1))
                    else:
                        done(f"{s} ulo{t}{b}", ins)

            def scale_gate(s, l, m, i=None):
                dve.wait_ge(cell_filled, ffn_value(s, l, m) + by(i, 4))
                dve.wait_ge(h_ready, ffn_value(s, l, m - 2, 4) + by(i, 4))
                if m == TM_CELLS:
                    wait(AC, f"{s} rr", l)
                dve.tensor_tensor(gate[:, m % 2, :], ps[:, m % 4, 0:UW], rrow_f[:, :], ALU.mult).then_inc(gate_scaled, 1)

            def product(s, l, m, i=None):
                dve.wait_ge(gate_ready, ffn_value(s, l, m) + by(i, 4))
                dve.wait_ge(hT_lo, ffn_value(s, l, m - 2, 2) + by(i, 4))
                dve.tensor_tensor(hh[:, m % 2, :], ps[:, m % 4, UW:2 * UW], gate[:, m % 2, :],
                                  ALU.mult).then_inc(h_ready, 1)

            def enter(l, s, before, n):
                residual(l, before, n, 0)
                split(s, l, 0)
                norm_lo(l, s, 0)
                split(s, l, 1)
                split(s, l, 2)
                residual(l, before, n, 1)
                enter_rest(l, s)

            def enter_rest(l, s):
                split(s, l, 3)
                if s != "m":
                    product(s, l, 0)
                norm_lo(l, s, 1)

            def end_layer(l):
                residual(l, "f2", 2, 0)
                with dve.If(l < L - 1):
                    split("f1", l + 1, 0)
                norm_lo(l + 1, "f1", 0)
                with dve.If(l < L - 1):
                    split("f1", l + 1, 1)
                    split("f1", l + 1, 2)
                residual(l, "f2", 2, 1)

            def ffn(s, l):
                def h_lo_part(m, i=None):
                    dve.wait_ge(hT_hi, ffn_value(s, l, m) + by(i, 4))
                    if m < TM_CELLS:
                        u, t = cell_place(m)
                        hi, lo = (tile[:, 2 * u:2 * u + 2, t * P:(t + 1) * P] for tile in (h_hi, h_lo))
                        src = ps[:, 4 + m % 2, 0:UW].rearrange("p (k n) -> p k n", k=2)
                    else:
                        hi, lo = (tile[:, bass.ds(m + by(i, 4), 1), :] for tile in (h_hi, h_lo))
                        src = hh[:, m % 2, :].unsqueeze(1)
                    dve.tensor_tensor(lo, src, hi.bitcast(F32), ALU.subtract).then_inc(hT_lo, 1)

                def slot(n, i=None):
                    if 2 <= n <= CELLS and n - 1 < TM_CELLS:
                        product(s, l, n - 1, i)
                    if n - 1 >= TM_CELLS and n + 2 < FFN_CHUNKS:
                        split(s, l, n + 2, i)
                    if n <= CELLS and n - 1 >= TM_CELLS:
                        scale_gate(s, l, n - 1, i)
                    if 2 <= n <= CELLS + 1:
                        h_lo_part(n - 2, i)
                    if 4 <= n + 2 and n - 1 < TM_CELLS:
                        split(s, l, n + 2, i)
                    if n <= CELLS and n - 1 >= TM_CELLS:
                        product(s, l, n - 1, i)

                for n in range(6):
                    slot(n)
                with dve.Fori(0, 3) as i:
                    for n in range(6, 10):
                        slot(n, i)
                for n in range(18, FFN_CHUNKS - 2):
                    slot(n)

            def mixer(l):
                def item(name):
                    wait(PE, name, l)
                    return ps[:, work_bank(name), :]

                def cell(m):
                    wait(PE, f"cell{m}", l)
                    return ps[:, m % 4, :]

                def rotate(a_, t, m, before):
                    src = cell(m).rearrange("p (h n) -> p h n", n=64)
                    if before:
                        wait(PO, f"rot {before}", l)
                    if not before:
                        wait(PO, "m pre1", l)
                    wait(AC, "cos", l)
                    r = rstd[:, 2 + t:3 + t]
                    done(f"rotc {a_}{t}", dve.scalar_tensor_tensor(
                        tmp[:, 0, :].rearrange("p (h n) -> p h n", n=64), src, r,
                        cos[:, t, :].unsqueeze(1).broadcast_to([P, 2 * RH, 64]), ALU.mult, ALU.mult))
                    done(f"rot {a_}{t}", dve.scalar_tensor_tensor(
                        tmp[:, 1, :].rearrange("p (h n) -> p h n", n=64), src, r,
                        sin[:, t, :].unsqueeze(1).broadcast_to([P, 2 * RH, 64]), ALU.mult, ALU.mult))

                def softplus():
                    b = item("dtT")
                    for t in range(T):
                        o = slice(t * HEADS, (t + 1) * HEADS)
                        ins = dve.scalar_tensor_tensor(dtr[:, o], b[:, o], rstd[:, 2 + t:3 + t],
                                                       cur[:, CUR_DTB:CUR_DTB + HEADS], ALU.mult, ALU.add)
                    chain("dt in", l, ins)
                    chain("nab", l, dve.scalar_tensor_tensor(nab, dtr, -1.0, dtr, ALU.mult, ALU.min))

                def softplus2():
                    wait(AC, "ex", l)
                    chain("dmx", l, dve.tensor_scalar(dmx, dtr, 0.0, None, ALU.max))
                    chain("sp0", l, dve.tensor_scalar(z1, ex, 2.0, None, ALU.add))
                    chain("sp1", l, dve.reciprocal(z1, z1))
                    chain("sp2", l, dve.tensor_tensor(z1, z1, ex, ALU.mult))
                    chain("sp3", l, dve.tensor_tensor(z2, z1, z1, ALU.mult))
                    chain("sp4", l, dve.tensor_scalar(zq, z2, 1.0 / 15, None, ALU.mult))
                    for n in (13, 11, 9, 7, 5, 3):
                        chain(f"zq{n}", l, dve.scalar_tensor_tensor(zq, zq, 1.0 / n, z2, ALU.add, ALU.mult))
                    chain("sp5", l, dve.scalar_tensor_tensor(zq, zq, 1.0, z1, ALU.add, ALU.mult))
                    chain("dt", l, dve.scalar_tensor_tensor(dt, zq, 2.0, dmx, ALU.mult, ALU.add))
                    chain("da", l, dve.scalar_tensor_tensor(
                        da.rearrange("p (t h) -> p t h", t=T), dt.rearrange("p (t h) -> p t h", t=T), -1.0,
                        na[:, :].unsqueeze(1).broadcast_to([P, T, HEADS]), ALU.mult, ALU.mult))

                    chain("da hi", l, dve.tensor_copy(da_hi[:, :], da))
                    done("da lo", dve.tensor_tensor(da_lo[:, :], da, da_hi[:, :].bitcast(F32), ALU.subtract))

                def conv(m, free):
                    wait_steps(dve, l, [(PE, f"cell{m}")] + free)
                    src = tmp[:, 2 + m % 2, :]
                    chain(f"xr {m}", l, dve.tensor_tensor(
                        src.rearrange("p (f n) -> p f n", f=2), ps[:, m % 4, :].rearrange("p (f n) -> p f n", f=2),
                        rrow[:, :].unsqueeze(1).broadcast_to([P, 2, T * P]), ALU.mult))
                    for tap in range(3, -1, -1):
                        for f in range(2):
                            ft = 2 * (m - 4) + f
                            w = cur[:, CUR_CW + tap * 12 + ft:CUR_CW + tap * 12 + ft + 1]
                            o = tmp[:, m % 2, f * 256:(f + 1) * 256]
                            s_ = src[:, f * 256:(f + 1) * 256]
                            sh = 3 - tap
                            if tap == 3:
                                ins = dve.tensor_scalar(o, s_, w, cur[:, CUR_CB + ft:CUR_CB + ft + 1], ALU.mult, ALU.add)
                            else:
                                ins = dve.scalar_tensor_tensor(o[:, sh:256], s_[:, 0:256 - sh], w, o[:, sh:256],
                                                               ALU.mult, ALU.add)
                            if tap and f == 0:
                                done(f"conv {m} {tap}{f}", ins)
                            elif tap:
                                chain(f"conv {m} {tap}{f}", l, ins)
                    done(f"conv {m}", ins)

                def scores(c):
                    done(f"P{c}", dve.tensor_tensor(
                        pr[:, c, :, :], item(f"sc{c}").rearrange("p (h n) -> p h n", h=RH),
                        const[:, C_DM:C_DM + RH * P].rearrange("p (h n) -> p h n", h=RH), ALU.mult))

                def mix(c, q):
                    i = 4 * c + q
                    wait(AC, f"E{c}{q}", l)
                    done(f"M{c}{q}", dve.tensor_tensor(
                        em[:, i % 2, :, :], em[:, i % 2, :, :],
                        mcb[:, c, q // 2, :].unsqueeze(1).broadcast_to([P, 4, P]), ALU.mult))

                def add_y(c, g):
                    o = ys[:, c, g * 512:(g + 1) * 512]
                    b = item(f"yi{c}{g}")
                    wait(PO, f"skip{c}", l)
                    chain(f"y{c}{g}", l, dve.tensor_tensor(o, b, o, ALU.add))

                def add_state(g):
                    o = ys[:, 1, g * 512:(g + 1) * 512]
                    e = ed[:, HEADS + 8 * g:HEADS + 8 * g + 8].unsqueeze(2).broadcast_to([P, 8, HP])
                    chain(f"yx{g}", l, dve.tensor_tensor(
                        xdt[:, 0, g * 512:(g + 1) * 512].rearrange("p (h d) -> p h d", h=8),
                        item(f"yx{g}").rearrange("p (h d) -> p h d", h=8), e, ALU.mult))
                    chain(f"ya{g}", l, dve.tensor_tensor(o, o, xdt[:, 0, g * 512:(g + 1) * 512], ALU.add))

                def moments(t, half):
                    b = item(f"r{t}{half}")
                    for h in range(2):
                        n = f"bn{t}{2 * half + h}"
                        done(n, dve.bn_stats(bn[:, t, 2 * half + h, :], b[:, h * RV:(h + 1) * RV]))
                    wait(DV, n, l)
                    dve.sem_inc(dve_waited, 1)
                    for h in range(2):
                        n = f"mv{t}{2 * half + h}" if (half, h) != (1, 1) else f"mv{t}"
                        done(n, dve.bn_aggr(mv[:, t, 2 * half + h, :], bn[:, t, 2 * half + h, :]))

                def group_norm(t):
                    wait(PO, f"gn{t}", l)
                    for half in range(2):
                        for h in range(2):
                            hd = 2 * half + h
                            ins = dve.tensor_scalar(vr[:, t, hd * RV:(hd + 1) * RV],
                                                    ps[:, work_bank(f"r{t}{half}"), h * RV:(h + 1) * RV],
                                                    mv[:, t, hd, 0:1], grs[:, t, hd:hd + 1], ALU.subtract, ALU.mult)
                        done(f"rn{t}{half}", ins)

                def gated(a_, i):
                    t, half = i % 2, i // 2
                    o = (ys if a_ == "z" else vr)[:, t, half * 512:(half + 1) * 512]
                    wait(AC, f"{a_}{i}", l)
                    if a_ == "g":
                        wait(DV, f"rn{t}{half}", l)
                    done(f"{a_}{i}", dve.tensor_tensor(o, o, tmp[:, i, :], ALU.mult))

                def ssm_norm(t):
                    wait(PO, f"ssm rs{t}", l)
                    done(f"yn{t}", dve.tensor_scalar(ys[:, t, :], ys[:, t, :], rstd[:, 4 + t:5 + t], None, ALU.mult))

                def yT(a_, j):
                    wait(AC, f"{a_}T{j}", l)
                    b = ps[:, work_bank(f"{a_}T{j}"), :]
                    for kk in range(2):
                        k = 2 * j + kk
                        hi, lo, col = (y_hi, y_lo, CUR_SSM) if a_ == "y" else (u_hi, u_lo, CUR_RET)
                        ins = dve.scalar_tensor_tensor(lo[:, k, :], b[:, kk * 256:(kk + 1) * 256],
                                                       cur[:, col + k:col + k + 1], hi[:, k, :].bitcast(F32),
                                                       ALU.mult, ALU.subtract)
                    done(f"{a_}T{j}", ins)

                def sp_(n):
                    if 4 <= n + 2 < MIX_CHUNKS:
                        split("m", l, n + 2)

                dve.wait_ge(param_in, N_PARAM)
                dt_in = dtw_raw[:, bass.ds(l * (KD * HEADS), KD * HEADS)].rearrange("p (k h) -> p k h", k=KD)
                done("gt_r", dve.tensor_copy(gt_r[:, :], gt))
                chain("dtw hi", l, dve.tensor_copy(dtw[:, :, 0:HEADS], dt_in))
                done("dtw lo", dve.tensor_tensor(dtw[:, :, HEADS:], dt_in, dtw[:, :, 0:HEADS].bitcast(F32), ALU.subtract))
                sp_(0)
                rotate("q", 0, 0, None)
                sp_(1)
                rotate("k", 0, 1, "q0")
                sp_(2)
                rotate("q", 1, 2, "k0")
                sp_(3)
                rotate("k", 1, 3, "q1")
                softplus()
                sp_(4)
                sp_(5)
                conv(4, [(PO, "rot k1"), (PE, "qT1"), (AC, "rr")])
                conv(5, [(PE, "kT1")])
                sp_(6)
                conv(6, [(PE, "xT0")])
                sp_(7)
                scores(0)
                conv(7, [(PE, "xT1")])
                sp_(8)
                conv(8, [(PE, "xT2")])
                sp_(9)
                conv(9, [(PE, "xT3")])
                softplus2()
                scores(1)
                sp_(10)
                sp_(11)
                done("cb", dve.tensor_tensor(
                    mcb[:, :, :, :].rearrange("p c g n -> p (c g) n"), item("cb").rearrange("p (a n) -> p a n", a=4),
                    le.unsqueeze(1).broadcast_to([P, 4, P]), ALU.mult))
                wait(DV, "cb", l)
                mix(0, 0)
                sp_(12)
                mix(0, 1)
                sp_(13)
                mix(0, 2)
                add_y(0, 0)
                mix(0, 3)
                sp_(14)
                mix(1, 0)
                add_y(0, 1)
                sp_(15)
                mix(1, 1)
                add_y(1, 0)
                mix(1, 2)
                sp_(16)
                add_state(0)
                mix(1, 3)
                moments(0, 0)
                moments(0, 1)
                gated("z", 0)
                add_y(1, 1)
                sp_(17)
                add_state(1)
                group_norm(0)
                gated("z", 1)
                sp_(18)
                gated("z", 2)
                moments(1, 0)
                moments(1, 1)
                gated("z", 3)
                sp_(19)
                group_norm(1)
                gated("g", 0)
                ssm_norm(0)
                ssm_norm(1)
                sp_(20)
                gated("g", 1)
                yT("y", 0)
                yT("y", 1)
                sp_(21)
                gated("g", 2)
                sp_(22)
                gated("g", 3)
                yT("y", 2)
                yT("y", 3)
                yT("r", 0)
                yT("r", 1)
                sp_(23)
                yT("r", 2)
                yT("r", 3)
                for n in range(24, MIX_CHUNKS - 2):
                    sp_(n)

            dve.wait_ge(setup_act, 2)
            norm_lo(0, "f1", 0, ahead=True, halves=[0])
            for h in range(2):
                half = slice(h * CW // 2, (h + 1) * CW // 2)
                dve.wait_ge(hi_done if h else half_hi, 1)
                ins = dve.tensor_tensor(w_lo[:, 0, half], raw[:, 0, half], w_hi[:, 0, half].bitcast(F32), ALU.subtract)
            ins.then_inc(lo_done, 1)
            norm_lo(0, "f1", 0, ahead=True, halves=[1])
            for c in range(1, 3):
                split("f1", 0, c)
            with dve.Fori(0, L) as l:
                enter_rest(l, "f1")
                wait(DV, "f1 ulo11", l)
                wait(PE, "param T", l)
                done("cur next", dve.tensor_copy(cur[:, 0:8], ps[:, 5, bass.ds(l * 8 + 8, 8)]))
                done("cur cw", dve.tensor_copy(cur[:, CUR_CW:CUR_CW + 48], ps[:, 5, bass.ds(l * 48 + 104, 48)]))
                done("cur cb", dve.tensor_copy(cur[:, CUR_CB:CUR_CB + 12], ps[:, 5, bass.ds(l * 12 + 80, 12)]))
                for i in range(1, 5):
                    done(f"cur{i}", dve.tensor_copy(cur[:, 8 * i:8 * i + 8], ps[:, 5, bass.ds(l * 8 + 16 * i, 8)]))
                dve.wait_ge(param_in, N_PARAM)
                for i in range(2):
                    done(f"cur b{i}", dve.tensor_copy(cur[:, CUR_DTB + 16 * i:CUR_DTB + 16 * i + 16],
                                                      bcf_flat[:, bass.ds(l * 16 + 32 * i, 16)]))
                chain("cur", l, dve.tensor_copy(cur[:, CUR_DS:CUR_DS + 16], bcf_flat[:, bass.ds(l * 16 + 64, 16)]))
                ffn("f1", l)
                enter(l, "m", "f1", 0)
                mixer(l)
                enter(l, "f2", "m", 1)
                ffn("f2", l)
                end_layer(l)

        @block.tensor
        def _(pe):
            pe.sem_inc(weights_used, RING - 1)
            pe.wait_ge(setup_pool, 2)
            for _ in range(WARM_BEFORE_X):
                pe.matmul(ps[:, 7, :], zeros[:, 0:P], zeros[:, :], start=True, stop=True)
            pe.wait_ge(ident_in, 32)
            pe.transpose(ps[:, 0, 0:16], first_rows[:, :], ident[0:16, 0:16]).then_inc(setup_pe, 1)

            def wait(st, name, l):
                pe.wait_ge(st.sem, st.at(name, l))

            def three(out, s_hi, s_lo, m_hi, m_lo, start, stop, release=False):
                first = pe.matmul(out, s_hi, m_hi, start=start, stop=False)
                if release:
                    first.then_inc(weights_used, 1)
                pe.matmul(out, s_hi, m_lo, start=False, stop=False)
                return pe.matmul(out, s_lo, m_hi, start=False, stop=stop)

            def norm_transpose(l, s, t, ahead=False):
                pe.wait_ge(x_in[t], 16)
                if not ahead:
                    before, lb = {"f1": ("f2", l - 1), "m": ("f1", l), "f2": ("m", l)}[s]
                    wait(DV, f"{before} res{t}", lb)
                for b in range(2):
                    if ahead and b:
                        pe.wait_ge(x_in_half, 16)
                    for k in range(4):
                        kk = 4 * b + k
                        ins = pe.transpose(ps[:, 4 + 2 * t + b, k * P:(k + 1) * P], x[:, t, kk * P:(kk + 1) * P], ident)
                    name = f"{s} normT{t}{b}" if b == 0 else f"{s} normT{t}"
                    ins.then_inc(PE.sem, PE.ahead_of_loop(name, last=b == 1) if ahead else PE.tick(name))

            def after_unit(n):
                return n == 0 or n == 3 or (n >= 4 and n % 2 == 0)

            def cell(s, l, n):
                u, t = cell_place(n)
                c0, bank, last = 2 * u, n % 4, t == 1
                for kh in range(2):
                    if n == 1 and kh == 1:
                        norm_transpose(l, s, 1)
                    if n in (0, 2):
                        wait(DV, f"{s} ulo{t}{kh}", l)
                    c = c0 + kh
                    slot = slot_of(s, c)
                    pe.wait_ge(lo_done, chunk_value(s, l, c, RING))
                    for k in range(4):
                        kk = 4 * kh + k
                        cols = slice(k * 512, (k + 1) * 512)
                        ts = slice(t * P, (t + 1) * P)
                        ins = three(ps[:, bank, :], u_hi[:, kk, ts], u_lo[:, kk, ts], w_hi[:, slot, cols],
                                    w_lo[:, slot, cols], kk == 0, kk == KD - 1, after_unit(n) and kk == 0)
                    if last and kh == 0:
                        ins.then_inc(weights_used, 1)
                return ins

            def down(s, l, first, j, tts, stat, last, nj):
                c = first + j
                slot = slot_of(s, c)
                pe.wait_ge(lo_done, chunk_value(s, l, c, RING))
                for k in range(2):
                    kt = 2 * j + k
                    hi, lo, kk = stat(kt)
                    for t in tts:
                        ts = slice(t * P, (t + 1) * P)
                        st, en = kt == 0, kt == 2 * nj - 1
                        for n in range(2):
                            out = ps[:, 2 + 4 * t + n, :]
                            cols = slice(k * D + n * 512, k * D + (n + 1) * 512)
                            ins = three(out, hi[:, kk, ts], lo[:, kk, ts], w_hi[:, slot, cols],
                                        w_lo[:, slot, cols], st, en, kt == 0 and t == 0 and n == 0)
                if last and j < nj - 1:
                    ins.then_inc(weights_used, 1)
                return ins

            def down_tail(s, l, first, nj, stat, then):
                for t in range(T):
                    for j in range(nj - RING, nj):
                        if t == 1 and j == nj - 2 and then:
                            norm_transpose(l + (then == "f1"), then, 0)
                        ins = down(s, l, first, j, [t], stat, t == 1, nj)
                    ins.then_inc(PE.sem, PE.tick(f"{s} acc{t}"))

            def ffn(s, l, then):
                def token_cell(n):
                    pe.wait_ge(h_ready, ffn_value(s, l, n - 4, 4))
                    cell(s, l, n).then_inc(cell_filled, 1)

                def turn_h(m):
                    pe.wait_ge(h_ready, ffn_value(s, l, m, 4))
                    pe.wait_ge(hT_lo, ffn_value(s, l, m - 2, 2))
                    for k in range(2):
                        ins = pe.transpose(ps[:, 4 + m % 2, k * P:(k + 1) * P], hh[:, m % 2, k * P:(k + 1) * P], ident)
                    ins.then_inc(hT_filled, 1)

                def feature_cell(n, i=None):
                    u, f = n // 2, n % 2
                    pe.wait_ge(h_ready, ffn_value(s, l, n - 4, 4) + by(i, 4))
                    pe.wait_ge(lo_done, chunk_value(s, l, 2 * u + 1, RING) + by(i, 4))
                    for g in range(2):
                        for k in range(KD):
                            slot = slot_of(s, 2 * u + k // 4)
                            o = (k % 4) * 512 + g * UW + f * P
                            cols = slice(o, o + P)
                            ins = three(ps[:, n % 4, g * UW:(g + 1) * UW], w_hi[:, slot, cols], w_lo[:, slot, cols],
                                        u_hi[:, k, :], u_lo[:, k, :], k == 0, k == KD - 1,
                                        after_unit(n) and g == 0 and k == 0)
                            if f and g and k == 3:
                                ins.then_inc(weights_used, 1)
                    ins.then_inc(cell_filled, 1)

                token_cell(0)
                token_cell(1)
                if s == "f1":
                    pe.wait_ge(norm_rows_in, 16 * 7)
                    wait(DV, "f1 ulo01", l)
                    pe.transpose(ps[:, 5, 0:104], rows[:, :], ident[0:104, 0:104])
                    pe.transpose(ps[:, 5, 104:200], rows_w[:, :], ident[0:96, 0:96]).then_inc(PE.sem, PE.tick("param T"))
                turn_h(0)
                token_cell(2)
                if s == "f1":
                    wait(DV, "cur4", l)
                turn_h(1)
                wait(PO, f"{s} pre1", l)
                for t in range(T):
                    ins = pe.matmul(ps[:, 6, t * P:(t + 1) * P], rstd[:, 2 + t:3 + t].broadcast_to([P, P]), ident,
                                    start=True, stop=True)
                ins.then_inc(PE.sem, PE.tick(f"{s} rr"))
                token_cell(3)
                turn_h(2)
                feature_cell(4)
                turn_h(3)
                feature_cell(5)
                with pe.Fori(0, 4) as i:
                    for n in range(6, 10):
                        feature_cell(n, i)

                def stat(kt):
                    return h_hi, h_lo, kt

                nj = KF // 2
                pe.wait_ge(h_ready, ffn_value(s, l, CELLS - 3, 4))
                for j in range(nj - RING):
                    m = {0: 2, 1: 3}.get(j, 2 * j + 1)
                    pe.wait_ge(hT_lo, ffn_value(s, l, m, 2))
                    down(s, l, CELLS, j, range(T), stat, True, nj)
                pe.wait_ge(hT_lo, ffn_value(s, l, CELLS - 1, 2))
                down_tail(s, l, CELLS, nj, stat, then)

            def mixer(l):
                def work(name):
                    before = work_before(name)
                    need = [(S[before[1]], before[2])] if before else []
                    b = ps[:, work_bank(name), :]
                    kind, last = name[:2], None
                    if name == "rr":
                        wait_steps(pe, l, need + [(PO, "m pre1")])
                        for t in range(T):
                            last = pe.matmul(b[:, t * P:(t + 1) * P], rstd[:, 2 + t:3 + t].broadcast_to([P, P]), ident,
                                             start=True, stop=True)
                    elif name == "dt":
                        wait_steps(pe, l, need + [(DV, "dtw lo")])
                        for k in range(KD):
                            for u_ in (u_hi, u_lo):
                                last = pe.matmul(b[0:2 * HEADS, 0:T * P], dtw[:, k, :], u_[:, k, :],
                                                 start=k == 0 and u_ is u_hi, stop=k == KD - 1 and u_ is u_lo)
                    elif name == "dtT":
                        wait_steps(pe, l, need + [(AC, "dtf")])
                        for t in range(T):
                            last = pe.matmul(b[:, t * HEADS:(t + 1) * HEADS], dtf[:, t, :],
                                             const[0:2 * HEADS, C_SUM:C_SUM + HEADS], start=True, stop=True)
                    elif kind in ("qT", "kT"):
                        t = int(name[2])
                        wait_steps(pe, l, need + [(PO, f"rot {name[0]}{t}")])
                        for h in range(RH):
                            last = pe.transpose(b[:, h * P:(h + 1) * P],
                                                tmp[:, 2 + "qk".index(name[0]), h * P:(h + 1) * P], ident)
                    elif kind == "xT":
                        m = 4 + int(name[2])
                        wait_steps(pe, l, need + [(AC, f"silu {m}")])
                        for t in range(T):
                            for f in range(2):
                                last = pe.transpose(b[:, (2 * t + f) * P:(2 * t + f + 1) * P],
                                                    tmp[:, m % 2, f * 256 + t * P:f * 256 + (t + 1) * P], ident)
                    elif kind == "sc":
                        c = int(name[2])
                        cs = slice(c * P, (c + 1) * P)
                        wait_steps(pe, l, need + [(AC, f"qT{c}"), (AC, f"kT{c}")])
                        for h in range(RH):
                            last = pe.matmul(b[:, h * P:(h + 1) * P], kT[:, h, cs], qT[:, h, cs], start=True, stop=True)
                    elif name == "cb":
                        wait_steps(pe, l, need + [(AC, "silu 9")])
                        for c in range(T):
                            cs = slice(c * P, (c + 1) * P)
                            for g in range(GROUPS):
                                o = (c * GROUPS + g) * P
                                last = pe.matmul(b[:, o:o + P], bcf[:, g, cs], bcf[:, GROUPS + g, cs], start=True, stop=True)
                    elif name == "bT":
                        wait_steps(pe, l, need + [(AC, "silu 8")])
                        for g in range(GROUPS):
                            last = pe.transpose(b[:, g * P:(g + 1) * P], bcf[:, g, 0:P], ident)
                    elif name == "dsum":
                        wait_steps(pe, l, need + [(DV, "da")])
                        pe.matmul(b[:, 0:HEADS], gt, da[:, 0:HEADS], start=True, stop=True)
                        last = pe.matmul(b[:, HEADS:2 * HEADS], le, da[:, HEADS:2 * HEADS], start=True, stop=True)
                    elif kind == "df":
                        c, q = int(name[2]), int(name[3])
                        wait_steps(pe, l, need + [(PO, f"uda{c}{q} lo")])
                        for part in range(2):
                            last = pe.matmul(b, gt_r[:, :], uda(4 * c + q, part).rearrange("p h n -> p (h n)"),
                                             start=part == 0, stop=part == 1)
                    elif kind == "yi":
                        c, g = int(name[2]), int(name[3])
                        for q in range(2):
                            qq = 2 * g + q
                            own = [(DV, f"M{c}{qq}")]
                            wait_steps(pe, l, own if q else need + own + [(PO, f"xdt{c}")])
                            for h in range(4):
                                o = (4 * q + h) * HP
                                hd = g * 512 + o
                                last = pe.matmul(b[:, o:o + HP], em[:, qq % 2, h, :], xdt[:, c, hd:hd + HP],
                                                 start=True, stop=True)
                            if q == 0:
                                last.then_inc(PE.sem, PE.tick(name + "h"))
                    elif kind == "ss":
                        g = int(name[2])
                        wait_steps(pe, l, need + [(AC, "bT"), (PO, "xde")])
                        last = pe.matmul(b, btok[:, g, :], xde[:, g * 512:(g + 1) * 512], start=True, stop=True)
                    elif kind == "yx":
                        g = int(name[2])
                        wait_steps(pe, l, need + [(AC, f"ss{g}")])
                        last = pe.matmul(b, bcf[:, GROUPS + g, P:2 * P], state[:, g, :], start=True, stop=True)
                    elif kind == "rs":
                        i = int(name[2])
                        wait_steps(pe, l, need + [(PO, "kdt"), (AC, f"v{2 * i}")])
                        for h in range(2):
                            hd = 2 * i + h
                            last = pe.matmul(b[:, h * RV:(h + 1) * RV], kdt[:, hd, :], vr[:, 0, hd * RV:(hd + 1) * RV],
                                             start=True, stop=True)
                    elif kind in ("r0", "r1"):
                        c, half = int(name[1]), int(name[2])
                        own = [(DV, f"P{c}"), (AC, f"v{2 * half + c}")]
                        if c == 1:
                            own += [(PO, "qdT"), (AC, f"rs{half}")]
                        wait_steps(pe, l, need + own)
                        for h in range(2):
                            hd = 2 * half + h
                            o = b[:, h * RV:(h + 1) * RV]
                            last = pe.matmul(o, pr[:, c, hd, :], vr[:, c, hd * RV:(hd + 1) * RV], start=True, stop=c == 0)
                            if c == 1:
                                last = pe.matmul(o, qdT[:, hd, :], rstate[:, hd, :], start=False, stop=True)
                    elif kind in ("yT", "rT"):
                        j = int(name[2])
                        src = ys if kind == "yT" else vr
                        wait_steps(pe, l, need + [(DV, f"yn{t}" if kind == "yT" else f"g{2 * (j // 2) + t}")
                                                  for t in range(T)])
                        for kk in range(2):
                            for t in range(T):
                                k = 2 * j + kk
                                o = (2 * kk + t) * P
                                last = pe.transpose(b[:, o:o + P], src[:, t, k * P:(k + 1) * P], ident)
                    last.then_inc(PE.sem, PE.tick(name))

                for m in range(CELLS):
                    kind, i = MIX_CELL[m]
                    if m >= 4:
                        st, name = MIX_FREE[m - 4]
                        wait(S[st], name, l)
                    u, t = cell_place(m)
                    if kind in "xb":
                        half = m % 2
                        pe.wait_ge(lo_done, chunk_value("m", l, 2 * u + 1, RING))
                        for f in range(2):
                            for k in range(KD):
                                slot = slot_of("m", 2 * u + k // 4)
                                o = (k % 4) * 512 + (2 * half + f) * P
                                cols = slice(o, o + P)
                                ins = three(ps[:, m % 4, f * 256:(f + 1) * 256], w_hi[:, slot, cols], w_lo[:, slot, cols],
                                            u_hi[:, k, :], u_lo[:, k, :], k == 0, k == KD - 1,
                                            after_unit(m) and f == 0 and k == 0)
                                if half and f and k == 3:
                                    ins.then_inc(weights_used, 1)
                    else:
                        ins = cell("m", l, m)
                    ins.then_inc(PE.sem, PE.tick(f"cell{m}"))
                    for name in ORDER:
                        if AFTER.get(name) == m:
                            work(name)

                def stat(kt):
                    return (y_hi, y_lo, kt) if kt < KD else (u_hi, u_lo, kt - KD)

                wait(AC, "g1", l)
                for j in range(4):
                    wait(DV, f"yT{j}", l)
                    down("m", l, CELLS, j, range(T), stat, True, 8)
                    if j < 2:
                        for i in range(2):
                            work(f"rT{2 * j + i}")
                wait(DV, "rT3", l)
                down_tail("m", l, CELLS, 8, stat, "f2")

            norm_transpose(0, "f1", 0, ahead=True)
            for _ in range(WARM_AFTER_X):
                pe.matmul(ps[:, 7, :], zeros[:, 0:P], zeros[:, :], start=True, stop=True)
            with pe.Fori(0, L) as l:
                ffn("f1", l, "m")
                mixer(l)
                ffn("f2", l, "f1")

    return {e: s.result() for e, s in S.items()}


NAMES = ["x", "positions", "ffn1_pre_norm", "ffn1_w_in", "ffn1_w_out", "ffn1_post_norm", "mix_pre_norm",
         "mix_w_in", "conv_w", "conv_b", "dt_bias", "a_log", "d_skip", "ssm_norm", "ret_norm", "mix_w_out",
         "mix_post_norm", "ffn2_pre_norm", "ffn2_w_in", "ffn2_w_out", "ffn2_post_norm"]


def constants(np):
    c = np.zeros((P, N_CONST), np.float32)
    row, col = np.arange(P)[:, None], np.arange(P)[None, :]
    c[:, C_ID:C_ID + P] = row == col
    c[:, C_LE:C_LE + P] = row <= col
    c[:, C_GT:C_GT + P] = row > col
    scale = RK ** -0.5
    for h in range(RH):
        lg = np.log(1.0 - 2.0 ** (-5.0 - h))
        c[:, C_DM + h * P:C_DM + (h + 1) * P] = np.where(row <= col, np.exp((col - row) * lg), 0.0) * scale
        c[:, C_QD + h * P:C_QD + (h + 1) * P] = np.exp((col + 1.0) * lg)
        c[:, C_KD + h] = np.exp((P - 1.0 - row[:, 0]) * lg) * scale
    c[0:2 * HEADS, C_SUM:C_SUM + HEADS] = np.tile(np.eye(HEADS), (2, 1))
    c[:, C_IF:C_IF + 64] = 10000.0 ** (-np.arange(64) / 64)
    return c


def kernel(**inputs):
    import numpy as np
    import concourse.bacc as bacc
    from concourse.bass_utils import run_bass_kernel_spmd

    def build(known):
        nc = bacc.Bacc("TRN2", target_bir_lowering=False, num_devices=1)
        aps = {}
        for n, v in arrays.items():
            aps[n] = nc.dram_tensor(f"in_{n}", v.shape, mybir.dt.from_np(v.dtype), kind="ExternalInput").ap()
        aps["out"] = nc.dram_tensor("out", arrays["x"].shape, F32, kind="ExternalOutput").ap()
        return nc, trunk(nc, aps, known)

    arrays = {n: np.ascontiguousarray(inputs[n]) for n in NAMES}
    arrays["const"] = constants(np)
    _, steps = build(None)
    nc, _ = build(steps)
    r = run_bass_kernel_spmd(nc, [{f"in_{n}": v for n, v in arrays.items()}], core_ids=[0])
    return r.results[0]["out"]
```
